# Optimizing a Trainium2 kernel written in Bass

```python
import math
import jax, jax.numpy as jnp
from jax import lax
import numpy as np

D_MODEL = 1024
BATCH = 1
SEQ = 256
DEPTH = 1

GDN_HEADS = 8
GDN_DK = 128
GDN_DV = 128
GDN_CONV = 4
GDN_CHUNK = 64
MLA_HEADS = 8
MLA_Q_RANK = 384
MLA_KV_RANK = 256
MLA_NOPE = 128
MLA_ROPE = 64
MLA_V = 128
ROPE_THETA = 10000.0
Q_BLOCK = 128
D_FF = 2816
FFN_CONV = 3
EPS = 1e-6

SPLIT_SIZES = (
    3 * GDN_HEADS * GDN_DK if GDN_DK == GDN_DV else 2 * GDN_HEADS * GDN_DK + GDN_HEADS * GDN_DV,
    GDN_HEADS * GDN_DV,
    GDN_HEADS,
    GDN_HEADS,
    MLA_Q_RANK,
    MLA_KV_RANK,
    MLA_ROPE,
    D_MODEL,
    D_MODEL,
)
D_IN = sum(SPLIT_SIZES)


def rmsnorm(x, g):
    xf = x.astype(jnp.float32)
    xf = xf * lax.rsqrt(jnp.mean(xf * xf, axis=-1, keepdims=True) + EPS)
    return (xf * g.astype(jnp.float32)).astype(x.dtype)

def l2norm(x):
    return x * lax.rsqrt(jnp.sum(x * x, axis=-1, keepdims=True) + EPS)

def causal_dwconv(x, w):
    k = w.shape[0]
    return lax.conv_general_dilated(
        x, w[:, None, :].astype(x.dtype), window_strides=(1,), padding=[(k - 1, 0)],
        dimension_numbers=("NWC", "WIO", "NWC"), feature_group_count=x.shape[-1])

def split_in(z):
    offs = list(np.cumsum(SPLIT_SIZES)[:-1])
    return jnp.split(z, [int(o) for o in offs], axis=-1)

def rope(x, pos):
    half = x.shape[-1] // 2
    inv = ROPE_THETA ** (-jnp.arange(half, dtype=jnp.float32) / half)
    ang = pos.astype(jnp.float32)[:, None] * inv[None, :]
    cos = jnp.cos(ang)[:, None, :]
    sin = jnp.sin(ang)[:, None, :]
    xf = x.astype(jnp.float32)
    x1, x2 = xf[..., :half], xf[..., half:]
    return jnp.concatenate([x1 * cos - x2 * sin, x2 * cos + x1 * sin], axis=-1).astype(x.dtype)

def gdn_chunked(q, k, v, g, beta):
    b, s, h, dk = q.shape
    dv = v.shape[-1]
    c = GDN_CHUNK
    n = s // c
    f32 = jnp.float32
    q = l2norm(q.astype(f32)) * (dk ** -0.5)
    k = l2norm(k.astype(f32))
    v = v.astype(f32)

    def chunk(t):
        t = t.reshape((b, n, c, h) + t.shape[3:])
        return jnp.moveaxis(t, 3, 1)

    q, k, v = chunk(q), chunk(k), chunk(v)
    g = jnp.cumsum(chunk(g.astype(f32)), axis=-1)
    beta = chunk(beta.astype(f32))
    k_beta = k * beta[..., None]
    v_beta = v * beta[..., None]

    causal = jnp.tril(jnp.ones((c, c), dtype=bool))
    diff = g[..., :, None] - g[..., None, :]
    decay = jnp.where(causal, jnp.exp(jnp.where(causal, diff, 0.0)), 0.0)

    lmat = jnp.einsum("bhnid,bhnjd->bhnij", k_beta, k) * decay
    rhs = jnp.concatenate([v_beta, k_beta * jnp.exp(g)[..., None]], axis=-1)
    sol = lax.linalg.triangular_solve(lmat, rhs, left_side=True, lower=True, unit_diagonal=True)
    u, w = sol[..., :dv], sol[..., dv:]

    a_intra = jnp.einsum("bhnid,bhnjd->bhnij", q, k) * decay
    q_dec = q * jnp.exp(g)[..., None]
    k_dec = k * jnp.exp(g[..., -1:] - g)[..., None]
    g_last = jnp.exp(g[..., -1])

    xs = tuple(jnp.moveaxis(t, 2, 0) for t in (u, w, q_dec, k_dec, a_intra, g_last))

    def step(state, inp):
        u_n, w_n, qd_n, kd_n, a_n, gl_n = inp
        v_new = u_n - jnp.einsum("bhck,bhkv->bhcv", w_n, state)
        o = jnp.einsum("bhck,bhkv->bhcv", qd_n, state) + jnp.einsum("bhij,bhjv->bhiv", a_n, v_new)
        state = state * gl_n[..., None, None] + jnp.einsum("bhck,bhcv->bhkv", kd_n, v_new)
        return state, o

    s0 = jnp.zeros((b, h, dk, dv), dtype=f32)
    _, o = lax.scan(step, s0, xs)
    o = jnp.transpose(o, (1, 0, 3, 2, 4)).reshape(b, s, h, dv)
    return o

def mla_causal(q_nope, q_pe, k_nope, k_pe, v):
    s = q_nope.shape[1]
    scale = (MLA_NOPE + MLA_ROPE) ** -0.5
    outs = []
    for i in range(s // Q_BLOCK):
        q0, q1 = i * Q_BLOCK, (i + 1) * Q_BLOCK
        sc = (jnp.einsum("bqhd,bkhd->bhqk", q_nope[:, q0:q1], k_nope[:, :q1])
              + jnp.einsum("bqhr,bkr->bhqk", q_pe[:, q0:q1], k_pe[:, :q1]))
        sc = sc.astype(jnp.float32) * scale
        qpos = q0 + jnp.arange(Q_BLOCK)
        kpos = jnp.arange(q1)
        sc = jnp.where(qpos[:, None] >= kpos[None, :], sc, -jnp.inf)
        p = jax.nn.softmax(sc, axis=-1).astype(v.dtype)
        outs.append(jnp.einsum("bhqk,bkhd->bqhd", p, v[:, :q1]))
    return jnp.concatenate(outs, axis=1)

def first_inputs(seed: int = 0) -> dict:
    key = jax.random.key(seed)
    ks = jax.random.split(key, 24)
    L, D = DEPTH, D_MODEL
    nrm = lambda k, shape, fan: jax.random.normal(k, shape, jnp.float32) * (fan ** -0.5)
    gain = lambda k, n: 1.0 + 0.05 * jax.random.normal(k, (L, n), jnp.float32)
    a_log = jnp.log(jax.random.uniform(ks[3], (L, GDN_HEADS), jnp.float32, 1.0, 16.0))
    dt = jnp.exp(jax.random.uniform(ks[4], (L, GDN_HEADS), jnp.float32, math.log(1e-3), math.log(1e-1)))
    dt_bias = dt + jnp.log(-jnp.expm1(-dt))
    return {
        "x": jax.random.normal(ks[0], (BATCH, SEQ, D), jnp.float32),
        "norm_mix_g": gain(ks[1], D),
        "w_in": nrm(ks[2], (L, D, D_IN), D),
        "conv_qkv_w": nrm(ks[5], (L, GDN_CONV, SPLIT_SIZES[0]), GDN_CONV),
        "gdn_a_log": a_log,
        "gdn_dt_bias": dt_bias,
        "gdn_norm_g": gain(ks[6], GDN_DV),
        "mla_q_norm_g": gain(ks[7], MLA_Q_RANK),
        "w_uq": nrm(ks[8], (L, MLA_Q_RANK, MLA_HEADS * (MLA_NOPE + MLA_ROPE)), MLA_Q_RANK),
        "mla_kv_norm_g": gain(ks[9], MLA_KV_RANK),
        "w_ukv": nrm(ks[10], (L, MLA_KV_RANK, MLA_HEADS * (MLA_NOPE + MLA_V)), MLA_KV_RANK),
        "w_o_gdn": nrm(ks[11], (L, GDN_HEADS * GDN_DV, D), GDN_HEADS * GDN_DV),
        "w_o_mla": nrm(ks[12], (L, MLA_HEADS * MLA_V, D), MLA_HEADS * MLA_V),
        "w_out": nrm(ks[13], (L, D, D), D),
        "norm_ffn_g": gain(ks[14], D),
        "w_up": nrm(ks[15], (L, D, 2 * D_FF), D),
        "conv_ffn_w": nrm(ks[16], (L, FFN_CONV, 2 * D_FF), FFN_CONV),
        "w_down": nrm(ks[17], (L, D_FF, D), D_FF),
        "norm_final_g": 1.0 + 0.05 * jax.random.normal(ks[18], (D,), jnp.float32),
    }

def first_block(x, norm_mix_g, w_in, conv_qkv_w, gdn_a_log, gdn_dt_bias, gdn_norm_g,
              mla_q_norm_g, w_uq, mla_kv_norm_g, w_ukv, w_o_gdn, w_o_mla, w_out,
              norm_ffn_g, w_up, conv_ffn_w, w_down, norm_final_g):
    b, s, _ = x.shape
    pos = jnp.arange(s)
    hA, hB = GDN_HEADS, MLA_HEADS
    for l in range(DEPTH):
        h = rmsnorm(x, norm_mix_g[l])
        z = jnp.einsum("bsd,de->bse", h, w_in[l])
        qkv_a, gate_a, a_a, b_a, c_q, c_kv, k_pe, gate_br_a, gate_br_b = split_in(z)

        qkv_a = jax.nn.silu(causal_dwconv(qkv_a, conv_qkv_w[l]))
        q_a, k_a, v_a = jnp.split(qkv_a, [hA * GDN_DK, 2 * hA * GDN_DK], axis=-1)
        q_a = q_a.reshape(b, s, hA, GDN_DK)
        k_a = k_a.reshape(b, s, hA, GDN_DK)
        v_a = v_a.reshape(b, s, hA, GDN_DV)
        g_log = -jnp.exp(gdn_a_log[l].astype(jnp.float32)) * jax.nn.softplus(
            a_a.astype(jnp.float32) + gdn_dt_bias[l].astype(jnp.float32))
        beta = jax.nn.sigmoid(b_a.astype(jnp.float32))
        o_a = gdn_chunked(q_a, k_a, v_a, g_log, beta).astype(x.dtype)
        o_a = rmsnorm(o_a, gdn_norm_g[l]) * jax.nn.silu(gate_a.reshape(b, s, hA, GDN_DV))
        y_a = jnp.einsum("bse,ed->bsd", o_a.reshape(b, s, hA * GDN_DV), w_o_gdn[l])

        cq = rmsnorm(c_q, mla_q_norm_g[l])
        q_b = jnp.einsum("bsr,re->bse", cq, w_uq[l]).reshape(b, s, hB, MLA_NOPE + MLA_ROPE)
        q_nope, q_pe = q_b[..., :MLA_NOPE], rope(q_b[..., MLA_NOPE:], pos)
        ckv = rmsnorm(c_kv, mla_kv_norm_g[l])
        kv = jnp.einsum("bsr,re->bse", ckv, w_ukv[l]).reshape(b, s, hB, MLA_NOPE + MLA_V)
        k_nope, v_b = kv[..., :MLA_NOPE], kv[..., MLA_NOPE:]
        k_pe_r = rope(k_pe[:, :, None, :], pos)[:, :, 0, :]
        o_b = mla_causal(q_nope, q_pe, k_nope, k_pe_r, v_b)
        y_b = jnp.einsum("bse,ed->bsd", o_b.reshape(b, s, hB * MLA_V), w_o_mla[l])

        merged = jax.nn.sigmoid(gate_br_a) * y_a + jax.nn.sigmoid(gate_br_b) * y_b
        x = x + jnp.einsum("bsd,de->bse", merged, w_out[l])

        h = rmsnorm(x, norm_ffn_g[l])
        u = causal_dwconv(jnp.einsum("bsd,df->bsf", h, w_up[l]), conv_ffn_w[l])
        gate_f, up_f = u[..., :D_FF], u[..., D_FF:]
        x = x + jnp.einsum("bsf,fd->bsd", jax.nn.silu(gate_f) * up_f, w_down[l])
    return rmsnorm(x, norm_final_g)


DEPTH_2 = 2

GRID_W = 64
CTX_LEN = 256
N_MIXERS = 2
N_A = (DEPTH_2 + 1) // 2
N_B = DEPTH_2 // 2
D_MIX = D_MODEL
CHUNK = 128
CM_GROUPS = 8
CM_GROUP_DIM = D_MIX // CM_GROUPS
SSM_GROUP = 16
SSM_GROUPS = D_MIX // SSM_GROUP
SSM_STATE = 64
PEER_HEADS = 8
PEER_KEYS = 128
PEER_EXPERTS = PEER_KEYS * PEER_KEYS
PEER_TOPK = 16
PEER_DKEY = 512
PEER_DHALF = PEER_DKEY // 2
PEER_BLOCK = 128
N_MOD = 6


def _rmsnorm(x, g):
    x32 = x.astype(jnp.float32)
    y = x32 * lax.rsqrt(jnp.mean(x32 * x32, axis=-1, keepdims=True) + EPS)
    return (y * g.astype(jnp.float32)).astype(x.dtype)

def _layernorm(x, g, b):
    x32 = x.astype(jnp.float32)
    mu = jnp.mean(x32, axis=-1, keepdims=True)
    xc = x32 - mu
    y = xc * lax.rsqrt(jnp.mean(xc * xc, axis=-1, keepdims=True) + EPS)
    return (y * g.astype(jnp.float32) + b.astype(jnp.float32)).astype(x.dtype)

def _modulate(h, shift, scale):
    return h * (1.0 + scale) + shift

def _sincos_1d(pos, dim):
    omega = 1.0 / (10000.0 ** (jnp.arange(dim // 2, dtype=jnp.float32) / (dim // 2)))
    ang = pos[:, None] * omega[None, :]
    return jnp.concatenate([jnp.sin(ang), jnp.cos(ang)], axis=-1)

def _pos_embed_2d(rows, dim):
    r = jnp.repeat(jnp.arange(rows, dtype=jnp.float32), GRID_W)
    col = jnp.tile(jnp.arange(GRID_W, dtype=jnp.float32), rows)
    return jnp.concatenate([_sincos_1d(r, dim // 2), _sincos_1d(col, dim // 2)], axis=-1)

def _chunk_mixer(h, w_in, ln_g, ln_b, w_s, b_s, w_out):
    bsz, length, _ = h.shape
    z = jax.nn.gelu(h @ w_in)
    u, v = jnp.split(z, 2, axis=-1)
    v = _layernorm(v, ln_g, ln_b)
    v = v.reshape(bsz, length // CHUNK, CHUNK, CM_GROUPS, CM_GROUP_DIM)
    v = jnp.einsum("hpq,bnqhd->bnphd", w_s, v) + b_s.T[:, :, None]
    return (u * v.reshape(bsz, length, D_MIX)) @ w_out

def _cmul(ar, ai, br, bi):
    return ar * br - ai * bi, ar * bi + ai * br

def _scan_combine(e1, e2):
    a1r, a1i, b1r, b1i = e1
    a2r, a2i, b2r, b2i = e2
    ar, ai = _cmul(a2r, a2i, a1r, a1i)
    br, bi = _cmul(a2r, a2i, b1r, b1i)
    return ar, ai, br + b2r, bi + b2i

def _diag_scan(a_r, a_i, bu_r, bu_i, h0=None):
    if h0 is not None:
        inj_r, inj_i = _cmul(a_r, a_i, h0[0], h0[1])
        bu_r = bu_r.at[0].add(inj_r)
        bu_i = bu_i.at[0].add(inj_i)
    a_full_r = jnp.broadcast_to(a_r, bu_r.shape)
    a_full_i = jnp.broadcast_to(a_i, bu_i.shape)
    _, _, h_r, h_i = lax.associative_scan(_scan_combine, (a_full_r, a_full_i, bu_r, bu_i), axis=0)
    return h_r, h_i

def _ssm_direction(u_lat, u_ctx, a_r, a_i, bb_r, bb_i, c_r, c_i, need_ctx_out):
    def inject(u):
        return (jnp.einsum("lgc,gpc->lgp", u, bb_r), jnp.einsum("lgc,gpc->lgp", u, bb_i))

    def readout(h_r, h_i):
        return jnp.einsum("lgp,gcp->lgc", h_r, c_r) - jnp.einsum("lgp,gcp->lgc", h_i, c_i)

    hc_r, hc_i = _diag_scan(a_r, a_i, *inject(u_ctx))
    hx_r, hx_i = _diag_scan(a_r, a_i, *inject(u_lat), h0=(hc_r[-1], hc_i[-1]))
    if need_ctx_out:
        return readout(hx_r, hx_i), readout(hc_r, hc_i)
    return readout(hx_r, hx_i), None

def _ssm_mixer(xn, cn, w_in, lam_re, lam_im, log_step, b_re, b_im, c_re, c_im, d_skip, w_out,
               need_ctx_out):
    u_x = xn @ w_in
    u_c = cn @ w_in
    lr = lam_re.astype(jnp.float32)
    li = lam_im.astype(jnp.float32)
    step = jnp.exp(log_step.astype(jnp.float32))[..., None]
    mag = jnp.exp(lr * step)
    a_r = mag * jnp.cos(li * step)
    a_i = mag * jnp.sin(li * step)
    den = lr * lr + li * li
    coef_r = ((a_r - 1.0) * lr + a_i * li) / den
    coef_i = (a_i * lr - (a_r - 1.0) * li) / den
    bb_r, bb_i = _cmul(coef_r[..., None], coef_i[..., None],
                       b_re.astype(jnp.float32), b_im.astype(jnp.float32))
    c_r = c_re.astype(jnp.float32)
    c_i = c_im.astype(jnp.float32)

    def per_sample(args):
        ux, uc = args
        ux = ux.astype(jnp.float32).reshape(-1, SSM_GROUPS, SSM_GROUP)
        uc = uc.astype(jnp.float32).reshape(-1, SSM_GROUPS, SSM_GROUP)
        yf_x, yf_c = _ssm_direction(ux, uc, a_r[0], a_i[0], bb_r[0], bb_i[0], c_r[0], c_i[0],
                                    need_ctx_out)
        yb_x, yb_c = _ssm_direction(ux[::-1], uc[::-1], a_r[1], a_i[1], bb_r[1], bb_i[1],
                                    c_r[1], c_i[1], need_ctx_out)
        y_lat = yf_x + yb_x[::-1]
        if need_ctx_out:
            return y_lat, yf_c + yb_c[::-1]
        return y_lat

    out = lax.map(per_sample, (u_x, u_c))

    def finish(y, u):
        y = y.reshape(u.shape).astype(u.dtype) + d_skip * u
        val, gate = jnp.split(jax.nn.gelu(y) @ w_out, 2, axis=-1)
        return val * jax.nn.sigmoid(gate)

    if need_ctx_out:
        return finish(out[0], u_x), finish(out[1], u_c)
    return finish(out, u_x), None

def _peer(h, w_q, sub_keys, u_tab, v_tab):
    shape = h.shape
    blocks = h.reshape(-1, PEER_BLOCK, D_MODEL)

    def block(hb):
        q = (hb @ w_q).reshape(PEER_BLOCK, PEER_HEADS, 2, PEER_DHALF)
        s = jnp.einsum("nhkd,hkmd->nhkm", q.astype(jnp.float32), sub_keys.astype(jnp.float32))
        s_half, i_half = lax.top_k(s, PEER_TOPK)
        cand = s_half[:, :, 0, :, None] + s_half[:, :, 1, None, :]
        top_s, top_c = lax.top_k(cand.reshape(PEER_BLOCK, PEER_HEADS, PEER_TOPK * PEER_TOPK),
                                 PEER_TOPK)
        k1 = jnp.take_along_axis(i_half[:, :, 0], top_c // PEER_TOPK, axis=-1)
        k2 = jnp.take_along_axis(i_half[:, :, 1], top_c % PEER_TOPK, axis=-1)
        ids = k1 * PEER_KEYS + k2
        g = jax.nn.softmax(top_s, axis=-1)
        ue = jnp.take(u_tab, ids, axis=0)
        ve = jnp.take(v_tab, ids, axis=0)
        act = jax.nn.gelu(jnp.einsum("nd,nhkd->nhk", hb, ue).astype(jnp.float32))
        return jnp.einsum("nhk,nhkd->nd", (g * act).astype(hb.dtype), ve)

    return lax.map(block, blocks).reshape(shape)

def second_inputs(seed: int = 0) -> dict:
    key = jax.random.key(seed)
    ks = jax.random.split(key, 32)
    f32 = jnp.float32
    nrm = lambda k, s, std: jax.random.normal(k, s, f32) * std
    G, P = SSM_GROUPS, SSM_STATE
    lam_im0 = jnp.broadcast_to(jnp.pi * jnp.arange(P, dtype=f32), (N_B, 2, G, P))
    return {
        "x": nrm(ks[0], (BATCH, SEQ, D_MODEL), 1.0),
        "c": nrm(ks[1], (BATCH, D_MODEL), 1.0),
        "ctx": nrm(ks[2], (BATCH, CTX_LEN, D_MODEL), 1.0),
        "c_ctx": nrm(ks[3], (D_MODEL,), 1.0),
        "ada_w": nrm(ks[4], (DEPTH_2, D_MODEL, N_MOD * D_MODEL), 0.5 * D_MODEL ** -0.5),
        "ada_b": nrm(ks[5], (DEPTH_2, N_MOD * D_MODEL), 0.02),
        "norm1_g": 1.0 + nrm(ks[6], (DEPTH_2, D_MODEL), 0.02),
        "norm2_g": 1.0 + nrm(ks[7], (DEPTH_2, D_MODEL), 0.02),
        "final_g": 1.0 + nrm(ks[8], (D_MODEL,), 0.02),
        "cm_w_in": nrm(ks[9], (N_A, D_MODEL, 2 * D_MIX), D_MODEL ** -0.5),
        "cm_ln_g": 1.0 + nrm(ks[10], (N_A, D_MIX), 0.02),
        "cm_ln_b": nrm(ks[11], (N_A, D_MIX), 0.02),
        "cm_w_s": nrm(ks[12], (N_A, CM_GROUPS, CHUNK, CHUNK), CHUNK ** -0.5),
        "cm_b_s": 1.0 + nrm(ks[13], (N_A, CM_GROUPS, CHUNK), 0.02),
        "cm_w_out": nrm(ks[14], (N_A, D_MIX, D_MODEL), D_MIX ** -0.5),
        "ssm_w_in": nrm(ks[15], (N_B, D_MODEL, D_MIX), D_MODEL ** -0.5),
        "ssm_lam_re": -0.5 + nrm(ks[16], (N_B, 2, G, P), 0.01),
        "ssm_lam_im": lam_im0 + nrm(ks[17], (N_B, 2, G, P), 0.01),
        "ssm_log_step": jax.random.uniform(ks[18], (N_B, 2, G), f32,
                                           minval=math.log(1e-3), maxval=math.log(1e-1)),
        "ssm_b_re": nrm(ks[19], (N_B, 2, G, P, SSM_GROUP), (2 * SSM_GROUP) ** -0.5),
        "ssm_b_im": nrm(ks[20], (N_B, 2, G, P, SSM_GROUP), (2 * SSM_GROUP) ** -0.5),
        "ssm_c_re": nrm(ks[21], (N_B, 2, G, SSM_GROUP, P), P ** -0.5),
        "ssm_c_im": nrm(ks[22], (N_B, 2, G, SSM_GROUP, P), P ** -0.5),
        "ssm_d": nrm(ks[23], (N_B, D_MIX), 1.0),
        "ssm_w_out": nrm(ks[24], (N_B, D_MIX, 2 * D_MODEL), D_MIX ** -0.5),
        "peer_w_q": nrm(ks[25], (DEPTH_2, D_MODEL, PEER_HEADS * PEER_DKEY), D_MODEL ** -0.5),
        "peer_keys": nrm(ks[26], (DEPTH_2, PEER_HEADS, 2, PEER_KEYS, PEER_DHALF), PEER_DHALF ** -0.5),
        "peer_u": nrm(ks[27], (DEPTH_2, PEER_EXPERTS, D_MODEL), D_MODEL ** -0.5),
        "peer_v": nrm(ks[28], (DEPTH_2, PEER_EXPERTS, D_MODEL), (PEER_HEADS * PEER_TOPK) ** -0.5),
    }

def second_block(x, c, ctx, c_ctx, ada_w, ada_b, norm1_g, norm2_g, final_g,
              cm_w_in, cm_ln_g, cm_ln_b, cm_w_s, cm_b_s, cm_w_out,
              ssm_w_in, ssm_lam_re, ssm_lam_im, ssm_log_step, ssm_b_re, ssm_b_im,
              ssm_c_re, ssm_c_im, ssm_d, ssm_w_out,
              peer_w_q, peer_keys, peer_u, peer_v):
    rows = x.shape[1] // GRID_W
    x = x + _pos_embed_2d(rows, D_MODEL).astype(x.dtype)[None]
    h_ctx = ctx
    silu_c = jax.nn.silu(c)
    silu_cc = jax.nn.silu(c_ctx)
    for i in range(DEPTH_2):
        last = i == DEPTH_2 - 1
        k = i // N_MIXERS
        use_chunk = (i % N_MIXERS) == 0
        need_ctx_mix = (not last) or (not use_chunk)
        mod_x = (silu_c @ ada_w[i] + ada_b[i])[:, None, :]
        mod_c = (silu_cc @ ada_w[i] + ada_b[i])[None, None, :]
        sh1, sc1, g1, sh2, sc2, g2 = jnp.split(mod_x, N_MOD, axis=-1)
        csh1, csc1, cg1, csh2, csc2, cg2 = jnp.split(mod_c, N_MOD, axis=-1)

        xn = _modulate(_rmsnorm(x, norm1_g[i]), sh1, sc1)
        cn = _modulate(_rmsnorm(h_ctx, norm1_g[i]), csh1, csc1) if need_ctx_mix else None
        if use_chunk:
            y_x = _chunk_mixer(xn, cm_w_in[k], cm_ln_g[k], cm_ln_b[k], cm_w_s[k], cm_b_s[k],
                               cm_w_out[k])
            y_c = None if last else _chunk_mixer(cn, cm_w_in[k], cm_ln_g[k], cm_ln_b[k],
                                                 cm_w_s[k], cm_b_s[k], cm_w_out[k])
        else:
            y_x, y_c = _ssm_mixer(xn, cn, ssm_w_in[k], ssm_lam_re[k], ssm_lam_im[k],
                                  ssm_log_step[k], ssm_b_re[k], ssm_b_im[k], ssm_c_re[k],
                                  ssm_c_im[k], ssm_d[k], ssm_w_out[k], not last)
        x = x + g1 * y_x
        x = x + g2 * _peer(_modulate(_rmsnorm(x, norm2_g[i]), sh2, sc2),
                           peer_w_q[i], peer_keys[i], peer_u[i], peer_v[i])
        if not last:
            h_ctx = h_ctx + cg1 * y_c
            h_ctx = h_ctx + cg2 * _peer(_modulate(_rmsnorm(h_ctx, norm2_g[i]), csh2, csc2),
                                        peer_w_q[i], peer_keys[i], peer_u[i], peer_v[i])
    return _rmsnorm(x, final_g)


def setup_inputs(seed=0):
    out = dict(first_inputs(seed))
    for name, value in second_inputs(seed + 1).items():
        if name != "x":
            out[name + "_2"] = value
    return out


def reference(
    x, norm_mix_g, w_in, conv_qkv_w, gdn_a_log, gdn_dt_bias, gdn_norm_g, mla_q_norm_g, w_uq,
    mla_kv_norm_g, w_ukv, w_o_gdn, w_o_mla, w_out, norm_ffn_g, w_up, conv_ffn_w, w_down,
    norm_final_g, c_2, ctx_2, c_ctx_2, ada_w_2, ada_b_2, norm1_g_2, norm2_g_2, final_g_2,
    cm_w_in_2, cm_ln_g_2, cm_ln_b_2, cm_w_s_2, cm_b_s_2, cm_w_out_2, ssm_w_in_2, ssm_lam_re_2,
    ssm_lam_im_2, ssm_log_step_2, ssm_b_re_2, ssm_b_im_2, ssm_c_re_2, ssm_c_im_2, ssm_d_2,
    ssm_w_out_2, peer_w_q_2, peer_keys_2, peer_u_2, peer_v_2,
):
    x = first_block(
        x, norm_mix_g, w_in, conv_qkv_w, gdn_a_log, gdn_dt_bias, gdn_norm_g, mla_q_norm_g, w_uq,
        mla_kv_norm_g, w_ukv, w_o_gdn, w_o_mla, w_out, norm_ffn_g, w_up, conv_ffn_w, w_down,
        norm_final_g,
    )
    return second_block(
        x, c_2, ctx_2, c_ctx_2, ada_w_2, ada_b_2, norm1_g_2, norm2_g_2, final_g_2, cm_w_in_2,
        cm_ln_g_2, cm_ln_b_2, cm_w_s_2, cm_b_s_2, cm_w_out_2, ssm_w_in_2, ssm_lam_re_2,
        ssm_lam_im_2, ssm_log_step_2, ssm_b_re_2, ssm_b_im_2, ssm_c_re_2, ssm_c_im_2, ssm_d_2,
        ssm_w_out_2, peer_w_q_2, peer_keys_2, peer_u_2, peer_v_2,
    )


_drawn_inputs = setup_inputs


def setup_inputs(seed=0):
    import zlib

    import numpy as np

    out = dict(_drawn_inputs(seed))
    spreads = {}
    factors = {'gdn_norm_g': 3.792,
     'mla_q_norm_g': 8.0,
     'mla_kv_norm_g': 7.974,
     'ctx_2': 64.0,
     'c_ctx_2': 64.0,
     'ada_b_2': 2.897,
     'norm1_g_2': 8.0,
     'norm2_g_2': 8.0,
     'final_g_2': 7.37,
     'cm_ln_g_2': 8.0,
     'cm_ln_b_2': 8.0,
     'cm_b_s_2': 8.0,
     'ssm_lam_re_2': 64.0,
     'ssm_lam_im_2': 27.096,
     'ssm_log_step_2': 37.6,
     'ssm_b_re_2': 40.2,
     'ssm_b_im_2': 43.168,
     'ssm_c_re_2': 41.184,
     'ssm_c_im_2': 39.248,
     'peer_w_q_2': 3.431,
     'peer_keys_2': 3.439,
     'peer_u_2': 3.793,
     'peer_v_2': 3.412}
    for name, (base, spread) in spreads.items():
        noise = np.random.default_rng([zlib.crc32(name.encode()), seed]).standard_normal(out[name].shape)
        drawn = base * np.exp(spread * noise) if base else spread * noise
        out[name] = __import__('jax').numpy.asarray(drawn.astype(out[name].dtype))
    for name, factor in factors.items():
        out[name] = (out[name] * factor).astype(out[name].dtype)
    return out
```

```python
from contextlib import ExitStack

import numpy as np
import concourse.bass as bass
from concourse import mybir

F32 = mybir.dt.float32
U32 = mybir.dt.uint32
ALU = mybir.AluOpType
ACT = mybir.ActivationFunctionType
AX = mybir.AxisListType.X

P = 128
D = 1024
KD_ = D // P
S = 256
EPS = 1e-6
NH = 8
FT = 44
FK = 22
RING = 4
SLOT = 1024
NEXP = 128
TOPK = 16
NG = 64
NCH = 32
LEVELS = 7
LOWEST = -3.0e38
TWO_PI = 6.283185307179586
C1, C2 = 6.28125, 0.0019350051879882812
C3 = TWO_PI - C1 - C2
MAGIC = 12582912.0

COLS, _n = {}, 0
for _name, _w in (("ident", P), ("ones", P), ("iota", P), ("norm_mix", 8), ("conv", 96), ("gdn_norm", 1),
                  ("a_log", 1), ("dt_bias", 1), ("q_norm", 3), ("kv_norm", 2), ("norm_ffn", 8),
                  ("conv_ffn", 132), ("norm_final", 8), ("ada_b", 96), ("norm1", 16), ("norm2", 16),
                  ("final", 8), ("ln_g", 8), ("ln_b", 8), ("ssm_d", 8), ("cond", 16)):
    COLS[_name] = (_n, _w)
    _n += _w
NCOLS = _n
COLS1, _n = {}, 0
for _name, _w in (("cos", S), ("sin", S), ("neg", P), ("causal", P), ("levels", LEVELS * P), ("sel", NH * P)):
    COLS1[_name] = (_n, _w)
    _n += _w
NCOLS1 = _n

SEGS, _n = {}, 0
for _name, _w in (("in", 56), ("o_gdn", 8), ("uq", 6), ("kn", 2), ("v", 2), ("o_mla", 8), ("out", 8),
                  ("up", FT), ("down", FK), ("ada", 96), ("cm_in", 16), ("ws", 1), ("cm_out", 8),
                  ("q0", 32), ("keys0", 4), ("ssm_in", 8), ("ssm_out", 16), ("q1", 32), ("keys1", 4)):
    SEGS[_name] = (_n, _w)
    _n += _w
NSLOTS = _n


class Line:

    def __init__(self, eng, sem_of, chain):
        self.eng, self.sem_of, self.chain = eng, sem_of, chain
        self.base, self.k = 0, 0
        self.given, self.taken = {}, {}
        self.lin = 0
        self.slots = 0

    def do(self, ins):
        self.k += 1
        ins.then_inc(self.chain, 1)
        self.eng.wait_ge(self.chain, self.base + self.k)

    def give(self, ins, name):
        n = self.given[name] = self.given.get(name, 0) + 1
        ins.then_inc(self.sem_of(name), 1)
        self.eng.wait_ge(self.sem_of(name), n)

    def mark(self, ins, name):
        self.given[name] = self.given.get(name, 0) + 1
        ins.then_inc(self.sem_of(name), 1)

    def take(self, name):
        n = self.taken[name] = self.taken.get(name, 0) + 1
        self.eng.wait_ge(self.sem_of(name), n)

    def loop(self, count, per):
        start, b0 = self.k, self.base
        assert b0 == 0
        with self.eng.Fori(0, count) as i:
            self.base = start + i * per
            self.k = 0
            yield i
            assert self.k == per, (self.k, per)
        self.base, self.k = 0, start + count * per


def build(nc, io):
    ctx = ExitStack()
    with ctx:
        sems = {}

        def sem(name):
            if name not in sems:
                sems[name] = ctx.enter_context(nc.semaphore(name))
            return sems[name]

        sb = lambda name, shape, dt=F32: ctx.enter_context(nc.sbuf_tensor(name, shape, dt))
        ring = sb("ring", [P, RING, SLOT])
        X = sb("X", [P, KD_, 2 * S])[:, :, :]
        H = sb("H", [P, KD_, 2 * S])[:, :, :]
        arena = sb("arena", [P, 32768])
        small = sb("small", [P, 7800])
        psum = ctx.enter_context(nc.psum_tensor("psum", [P, 4096], F32))

        def view(t, off, *shape, parts=P):
            n = int(np.prod(shape))
            a = t[0:parts, off:off + n]
            if len(shape) == 2:
                return a.rearrange("p (a b) -> p a b", a=shape[0])
            if len(shape) == 3:
                return a.rearrange("p (a b c) -> p a b c", a=shape[0], b=shape[1])
            if len(shape) == 4:
                return a.rearrange("p (a b c d) -> p a b c d", a=shape[0], b=shape[1], c=shape[2])
            return a

        A = lambda off, *shape, parts=P: view(arena, off, *shape, parts=parts)
        PS = lambda off, *shape, parts=P: view(psum, off, *shape, parts=parts)
        bank = lambda b: psum[:, 512 * b:512 * b + 512]

        def col(name, k=0, n=1):
            o = COLS[name][0]
            return small[:, o + k:o + k + n]

        def col1(name, *shape, parts=P):
            o = NCOLS + COLS1[name][0]
            return view(small, o, *(shape or (COLS1[name][1],)), parts=parts)

        ident, ones, iota = col("ident", 0, P), col("ones", 0, P), col("iota", 0, P)
        T0 = 7800 - 1344
        assert NCOLS + NCOLS1 <= T0 and NCOLS + 4864 <= T0
        MOD = view(small, T0, 2, 48, 2)
        SA = view(small, T0 + 192, 2, 2, 8, 2)
        CS = view(small, T0 + 256, 8, 2)
        R1 = view(small, T0 + 272, 512)
        R2 = view(small, T0 + 784, 512)
        NGC = view(small, T0 + 1296, 2, 8)
        TSUM = view(small, T0 + 1312, 16)
        TMAX = view(small, T0 + 1328, 16)

        QKV = A(0, 24, S)
        Q_, K_, V_ = QKV[:, 0:8, :], QKV[:, 8:16, :], QKV[:, 16:24, :]
        SQ = A(6144, 16, S)
        TT = A(6144, 16, P)
        TI = A(8192, 16, P)
        OG = A(8192, 8, S)
        GT = A(10240, 8, S)
        GB = A(12288, 16, S)
        MISC = A(16384, 8, S)
        AB, CQ, CKV, KP, KPS = MISC[:, 0, :], MISC[:, 1:4, :], MISC[:, 4:6, :], MISC[:, 6, :], MISC[:, 7, :]
        BETA = A(18432, 8, S)
        ML = A(18432, 16, P)
        DEC = A(20480, 8, S)
        AM = A(20480, 16, P)
        EGB = A(22528, 8, P)
        EDB = A(23552, 8, P)
        VT = A(22528, 16, P)
        KDC = A(24576, 8, P)
        QD = A(25600, 8, P)
        KBG = A(26624, 8, P)
        LT = A(27648, 16, P)
        AT = A(29696, 16, P)
        ROWS = A(31744, 4, S, parts=8)
        VN0, VN1 = A(18432, 8, P), A(19456, 8, P)
        S1, RR = A(20480, 8, P), A(21504, 8, P)
        SQO = A(27648, 8, S)
        RSO = A(24576, 8, S)
        YA = A(0, 8, S)
        SQM = A(2048, 3, S)
        QN = A(4096, 8, S)
        QP = A(6144, 4, S)
        QPS = A(7168, 4, S)
        QPR = A(6144, 8, S)
        KN = A(8192, 8, S)
        MG = A(10240, 8, S)
        VM = A(18432, 2, D)
        SC = A(20480, 8, 384)
        PT = A(23552, 8, 384)
        OB = A(26624, 8, S)
        TMP = A(28672, 4, S)
        KPP = A(29696, 2, S)
        TME = A(28672, 2, S)
        UF = A(0, FT, S)
        SQX = A(12288, 8, S)
        SQX2 = A(0, 8, 2 * S)
        Z = A(0, 16, 512)
        SQZ = A(8192, 8, 512)
        ZT = A(12288, 32, P)
        BS = A(20480, D, parts=1)
        QT = A(0, 32, S)
        SCO = A(8192, 2, 16, P)
        SV = A(12288, 2, 16, 16)
        IDX = A(12800, 2, 16, 16).bitcast(U32)
        IDF = A(13312, 2, 16, 16)
        WK = A(13824, 256)
        CAND = A(14336, 16, 256)
        TS = A(18432, 16, 16)
        TC = A(18688, 16, 16).bitcast(U32)
        CI = A(18944, 2, 256).bitcast(U32)
        CF_ = A(19456, 2, 256)
        OH = A(20480, 256, 16)
        KK = A(24576, 3, 256)
        G = A(0, NEXP, S)
        E0 = NCOLS
        K3 = view(small, E0, 3, S)
        EA = view(small, E0 + 768, 2, 8, P)
        EB = view(small, E0 + 2816, 2, 8, P)
        AC = view(small, E0 + 768, 2, S)
        CF = view(small, E0 + 1280, 2, S)
        UT = A(0, 8, 512)
        UN = A(4096, NG, 8, 16, parts=64)
        XS = A(4096, 64, 2, NG)
        YN = A(4096, 8, D, parts=NCH)
        UG = A(12288, NG, 64)
        HS = A(16384, NCH, 2, NG)
        PW = A(20480, 9, 2, NG)
        PWI = A(21632, 2, NG, 8)
        PWM = A(22656, 2, NG, 15)
        PWO = A(24576, 2, NG, 8)
        BB = A(25600, 2, NG, 16)
        CC = A(27648, 3, NG, 16)
        RAW = A(30720, 2, NG, 16)
        TP = A(16384, 24, NG)
        LAM = A(16384 + 24 * NG, 3, NG)
        TB1, TB2 = A(18432, NG, 16), A(19456, NG, 16)
        W0 = NCOLS
        WW = view(small, W0, 2, 240)
        WC = view(small, W0 + 480, 2, P)
        WT1 = view(small, W0 + 736, 240)
        WT2 = view(small, W0 + 976, 240)
        STG = view(small, W0 + 1216, 2, P)
        STU = view(small, W0 + 1472, 3, NCH)
        HST = view(small, W0 + 1568, 2, 2, NG)
        ST1 = view(small, W0 + 1824, 2, NG)
        ST2 = view(small, W0 + 1952, 2, NG)
        A1C = view(small, W0 + 2080, 2, NG)
        A2C = view(small, W0 + 2208, 2, NG)
        YT = A(20480, 8, S)
        SG = A(22528, 8, S)
        TMPX = A(24576, 2, S)
        out_t = A(0, 8, S)

        nseg = lambda name: SEGS[name]

        stream = []

        def seg(*names):
            a = nseg(names[0])[0]
            b = nseg(names[-1])[0] + nseg(names[-1])[1]
            stream.append(("w", a, b - a))

        seg("in", "keys0")
        stream.append(("uv", 0, 0))
        seg("q0", "keys0")
        stream.append(("uv", 0, 0))
        seg("ssm_in", "keys1")
        stream.append(("uv", 1, 0))

        block = ctx.enter_context(nc.Block())

        @block.gpsimd
        def _(pool):
            pool.dma_start(H[:, :, S:2 * S], io["pos"]).then_inc(sem("pos_loaded"), 16)
            pool.wait_ge(sem("bs_room"), 1)
            pool.dma_start(BS, io["bs"]).then_inc(sem("bs_loaded"), 16)
            pool.wait_ge(sem("ssm_room"), 1)
            pool.dma_start(RAW, io["ssm_b"]).then_inc(sem("ssm_loaded"), 16)
            pool.dma_start(CC[:, 0:2], io["ssm_c"]).then_inc(sem("ssm_loaded"), 16)
            pool.dma_start(LAM, io["ssm_lam"]).then_inc(sem("ssm_loaded"), 16)

        @block.sync
        def _(sp):
            def load(dst, src, name="inputs_loaded"):
                sp.dma_start(dst, src).then_inc(sem(name), 16)

            load(X[:, :, 0:S], io["x"])
            load(small[:, 0:NCOLS], io["cols"])
            load(small[:, NCOLS:NCOLS + NCOLS1], io["cols1"])
            load(X[:, :, S:2 * S], io["ctx"])
            n = 0

            def slot(src, used, r):
                if used is not None:
                    sp.wait_ge(sem("slot_begun"), used)
                sp.dma_start(ring[:, r, :], src).then_inc(sem(f"slot_loaded{r}"), 16)

            def one(src, n):
                slot(src, n - RING + 2 if n >= RING else None, n % RING)

            for kind, a, count in stream:
                if kind == "w":
                    while count % RING or n < RING:
                        one(io["w"][a], n)
                        a, count, n = a + 1, count - 1, n + 1
                    with sp.Fori(0, count // RING) as i:
                        for b in range(RING):
                            slot(io["w"][i * RING + (a + b)], i * RING + (n + b - RING + 2), (n + b) % RING)
                    n += count
                else:
                    u, v = io["u"][a], io["v"][a]
                    one(u[0], n)
                    one(u[1], n + 1)
                    one(v[0], n + 2)
                    n += 3
                    with sp.Fori(0, (NEXP - 2) // 2) as i:
                        for b in range(2):
                            m = n + 2 * b
                            slot(u[i * 2 + (b + 2)], i * 4 + (m - RING + 2), m % RING)
                            slot(v[i * 2 + (b + 1)], i * 4 + (m - RING + 3), (m + 1) % RING)
                    n += 2 * (NEXP - 2)
                    one(v[NEXP - 1], n)
                    n += 1
            sp.wait_ge(sem("result_ready"), 1)
            load(io["out"], out_t, "result_stored")
            sp.wait_ge(sem("result_stored"), 16)

        @block.tensor
        def _(pe):
            L = Line(pe, sem, sem("pe_chain"))
            mm = pe.matmul

            def arrived(w):
                pe.wait_ge(sem(f"slot_loaded{w % RING}"), 16 * (w // RING + 1))

            def evacuated():
                pe.wait_ge(sem("lin_free"), L.lin)

            def linear(tiles, kt, rhs, n, m=P):
                w0, l0 = L.slots, L.lin
                if l0:
                    evacuated()
                begun = [False]

                def tile(t, static=True):
                    for k in range(kt):
                        s = t * kt + k
                        if s % 8 == 0:
                            begun[0] = True
                            if static:
                                arrived(w0 + s // 8)
                        last = mm(bank(t % 2)[0:m, 0:n], ring[:, (w0 + s // 8) % RING, (s % 8) * P:(s % 8) * P + m],
                                  rhs[:, k, 0:n], start=(k == 0), stop=(k == kt - 1))
                        if begun[0] and k < kt - 1:
                            last.then_inc(sem("slot_begun"), 1)
                            begun[0] = False
                    last.then_inc(sem("lin_ready"), 1)

                looped = kt == 8 and tiles % RING == 0 and tiles >= 8
                for t in range(RING if looped else tiles):
                    if t >= 2:
                        pe.wait_ge(sem("lin_free"), l0 + t - 1)
                    tile(t)
                if looped:
                    with pe.Fori(1, tiles // RING) as i:
                        for b in range(RING):
                            w = w0 + b
                            pe.wait_ge(sem("lin_free"), i * RING + (l0 + b - 1))
                            pe.wait_ge(sem(f"slot_loaded{w % RING}"), i * 16 + 16 * (w // RING + 1))
                            tile(b, False)
                assert not begun[0]
                L.lin += tiles
                L.slots += tiles * kt // 8

            def rowsum(src, kt, n, ready="squares"):
                if ready:
                    L.take(ready)
                for k in range(kt):
                    last = mm(bank(7)[:, 0:n], ones, src[:, k, 0:n], start=(k == 0), stop=(k == kt - 1))
                L.mark(last, "rowsum")

            pe.wait_ge(sem("inputs_loaded"), 64)
            rowsum(SQX, 8, S)
            L.take("normed")
            linear(24, 8, H, S)
            linear(8, 8, H, S)
            linear(8, 8, H, S)
            linear(16, 8, H, S)
            evacuated()
            L.take("head_squares")
            for b in range(8):
                last = mm(bank(b), ones, SQ[:, 2 * b:2 * b + 2, :], start=True, stop=True)
            L.mark(last, "head_sums")
            L.take("row_exps")
            L.take("head_sums_used")
            sel = col1("sel", NH, P, parts=8)
            for r in range(2):
                for h in range(NH):
                    last = mm(PS(2048 * r + S * h, S), sel[:, h, :], ROWS[:, r, :], start=(h % 2 == 0), stop=True,
                              skip_group_check=True)
            L.mark(last, "rows_spread")
            L.take("beta_evacuated")
            L.take("decay_evacuated")
            for h in range(NH):
                mm(PS(P * h, P), sel[:, h, :], ROWS[:, 2, P:S], start=(h % 4 == 0), stop=True, skip_group_check=True)
                mm(PS(1024 + P * h, P), sel[:, h, :], ROWS[:, 3, 0:P], start=(h % 4 == 0), stop=True,
                   skip_group_check=True)
            for c in range(2):
                last = pe.transpose(PS(2048 + 8 * c, 8), ROWS[:, 1, P * c:P * c + P], ident[0:8, 0:8])
            L.mark(last, "exps_spread")
            L.take("gdn_operands")
            for h in range(NH):
                for c in range(2):
                    j, t = 2 * h + c, slice(P * c, P * c + P)
                    mm(PS(P * j, P), K_[:, h, t], K_[:, h, t], start=(j % 4 == 0), stop=True, skip_group_check=True)
                    last = mm(PS(2048 + P * j, P), K_[:, h, t], Q_[:, h, t], start=(j % 4 == 0), stop=True,
                              skip_group_check=True)
            L.mark(last, "kk_ready")
            L.take("kk_evacuated")
            for h in range(NH):
                for c in range(2):
                    pe.transpose(PS(P * (2 * h + c), P), V_[:, h, P * c:P * c + P], ident)
                last = pe.transpose(PS(2048 + P * h, P), KDC[:, h, :], ident)
            L.mark(last, "vt_ready")
            L.take("vt_evacuated")
            L.take("inverse_begun")
            for j in range(16):
                last = pe.transpose(PS(P * j, P), TT[:, j, :], ident)
            L.mark(last, "inverse_turned")
            for lev in range(1, LEVELS):
                L.take("level_masked")
                for j in range(16):
                    last = mm(PS(P * j, P), ML[:, j, :], TI[:, j, :], start=(j % 4 == 0), stop=True,
                              skip_group_check=True)
                L.mark(last, "level_inner")
                L.take("level_inner_evacuated")
                for j in range(16):
                    if lev < LEVELS - 1:
                        mm(PS(2048 + P * j, P), TT[:, j, :], AM[:, j, :], start=(j % 4 == 0), stop=True,
                           skip_group_check=True)
                    last = mm(PS(P * j, P), AM[:, j, :], TT[:, j, :], start=(j % 4 == 0), stop=True,
                              skip_group_check=True)
                L.mark(last, "level_outer")
            L.take("inverse_ready")
            vt = VT.rearrange("p (h c) d -> p h c d", c=2)
            tt = TT.rearrange("p (h c) d -> p h c d", c=2)
            at = AT.rearrange("p (h c) d -> p h c d", c=2)

            def heads(off, *pairs):
                for h in range(NH):
                    for n, (a, b) in enumerate(pairs):
                        last = mm(PS(off + P * h, P), a[:, h, :], b[:, h, :], start=(h % 4 == 0 and n == 0),
                                  stop=(n == len(pairs) - 1), skip_group_check=True)
                return last

            L.mark(heads(0, (tt[:, :, 0, :], vt[:, :, 0, :])), "new0_ready")
            L.take("new0_evacuated")
            heads(1024, (KDC, VN0))
            L.mark(heads(2048, (VN0, at[:, :, 0, :])), "state_ready")
            L.take("state_evacuated")
            L.mark(heads(0, (KBG, S1)), "old_value_ready")
            L.take("residual_ready")
            L.mark(heads(1024, (tt[:, :, 1, :], RR)), "new1_ready")
            L.take("new1_evacuated")
            for h in range(NH):
                mm(PS(3072 + P * h, P), S1[:, h, :], QD[:, h, :], start=(h % 4 == 0), stop=False,
                   skip_group_check=True)
                last = mm(PS(3072 + P * h, P), VN1[:, h, :], at[:, h, 1, :], start=False, stop=True,
                          skip_group_check=True)
            L.mark(last, "gdn_out1")
            L.take("squares")
            for b in range(4):
                last = mm(bank(b), ones, SQO[:, 2 * b:2 * b + 2, :], start=True, stop=True)
            L.mark(last, "rowsum")
            L.take("gdn_gated")
            linear(8, 8, OG, S)
            rowsum(SQM, 3, S)
            rowsum(SQM, 2, S)
            L.take("latent_normed")
            linear(8, 3, CQ, S)
            linear(8, 3, CQ, S)
            linear(8, 2, CKV, S)
            for k in range(2):
                arrived(L.slots)
                for i in range(2):
                    for f in range(2):
                        last = mm(bank(2 + 2 * i + f), CKV[:, k, P * i:P * i + P],
                                  ring[:, L.slots % RING, 512 * f:512 * f + 512], start=(k == 0), stop=(k == 1))
                        if i == 0 and f == 0:
                            last.then_inc(sem("slot_begun"), 1)
                L.slots += 1
            L.mark(last, "v_ready")
            L.take("rope_ready")
            L.take("v_evacuated")
            evacuated()
            for h in range(NH):
                for c, (a, n) in enumerate(((0, P), (P, S))):
                    q = slice(P * c, P * c + P)
                    mm(bank(h)[:, a:a + n], QN[:, h, q], KN[:, h, 0:n], start=(c == 0), stop=False,
                       skip_group_check=True)
                    last = mm(bank(h)[:, a:a + n], QP[:, h // 2, q], KPP[:, h % 2, 0:n], start=False, stop=True,
                              skip_group_check=True)
            L.mark(last, "scores_ready")
            L.take("probs_ready")
            for h in range(NH):
                for j in range(3):
                    last = pe.transpose(bank(h)[:, P * j:P * j + P], SC[:, h, P * j:P * j + P], ident)
            L.mark(last, "probs_turned")
            L.take("probs_evacuated")
            for h in range(NH):
                v = slice(P * h, P * h + P)
                o = PS(S * h, S)
                mm(o[:, 0:P], VM[:, 0, v], PT[:, h, 0:P], start=(h % 2 == 0), stop=True, skip_group_check=True)
                mm(o[:, P:S], VM[:, 0, v], PT[:, h, P:S], start=False, stop=False, skip_group_check=True)
                last = mm(o[:, P:S], VM[:, 1, v], PT[:, h, S:S + P], start=False, stop=True, skip_group_check=True)
            L.mark(last, "attention_out")
            L.take("attention_ready")
            linear(8, 8, OB, S)
            linear(8, 8, MG, S)
            rowsum(SQX, 8, S)
            L.take("normed")
            linear(FT, 8, H, S)
            L.take("ffn_inner")
            linear(8, FK, UF, S)
            rowsum(SQX, 8, S)
            L.take("cond_silu")
            L.take("x_normed")
            w0 = L.slots

            def ada(t, b):
                o = psum[:, bass.ds(3072 + 2 * t, 2)]
                for k in range(8):
                    last = mm(o, ring[:, (w0 + b) % RING, P * k:P * k + P], CS[:, k, :], start=(k == 0),
                              stop=(k == 7), skip_group_check=True)
                    if k == 0:
                        last.then_inc(sem("slot_begun"), 1)
                return last

            with pe.Fori(0, 96 // RING - 1) as i:
                for b in range(RING):
                    w = w0 + b
                    pe.wait_ge(sem(f"slot_loaded{w % RING}"), i * 16 + 16 * (w // RING + 1))
                    ada(i * RING + b, b)
            for t in range(96 - RING, 96):
                arrived(w0 + t)
                last = ada(t, t)
            L.mark(last, "mods_ready")
            L.slots += 96

            def peer(p, off):
                linear(32, 8, H[:, :, off:off + S], S)
                evacuated()
                for s in range(4):
                    arrived(L.slots)
                    for q in range(4):
                        for i in range(2):
                            for d in range(2):
                                last = mm(bank(4 * i + s)[:, P * q:P * q + P],
                                          QT[:, 2 * (4 * s + q) + d, P * i:P * i + P],
                                          ring[:, L.slots % RING, P * (2 * q + d):P * (2 * q + d) + P],
                                          start=(q == 0 and d == 0), stop=(d == 1), skip_group_check=True)
                                if q == 0 and i == 0 and d == 0:
                                    last.then_inc(sem("slot_begun"), 1)
                    L.slots += 1
                L.mark(last, "key_scores")
                L.take("chosen")
                for m in range(3):
                    for i in range(2):
                        last = pe.transpose(PS(S * m + P * i, P), KK[:, m, P * i:P * i + P], ident)
                L.mark(last, "chosen_turned")
                L.take("chosen_evacuated")

                def build(n, b, first):
                    pe.wait_ge(sem("onehots_ready"), n + 1)
                    if not first:
                        pe.wait_ge(sem("gates_evacuated"), n - 1)
                    for t in range(8):
                        last = mm(PS(1024 * b + P * t, P), EB[:, b, t, :], EA[:, b, t, :], start=(t % 4 == 0),
                                  stop=True, skip_group_check=True)
                    last.then_inc(sem("gates_built"), 1)

                for b in range(2):
                    build(32 * p + b, b, True)
                with pe.Fori(1, 16) as i:
                    for b in range(2):
                        build(i * 2 + (32 * p + b), b, False)
                pe.wait_ge(sem("gates_evacuated"), 32 * p + 32)

                w0, n0 = L.slots, NEXP * p

                def up(j, b, r, wait, first=False):
                    wait()
                    if not first:
                        pe.wait_ge(sem("gelu_done"), j + (n0 - 1))
                    for k in range(8):
                        last = mm(bank(b)[:, 0:S], ring[:, r % RING, P * k:P * k + P], H[:, k, off:off + S],
                                  start=(k == 0), stop=(k == 7))
                        if k == 0:
                            last.then_inc(sem("slot_begun"), 1)
                    last.then_inc(sem("up_ready"), 1)

                def down(j, b, r, wait, first=False):
                    wait()
                    pe.wait_ge(sem("coef_ready"), j + (n0 + 1))
                    for d in range(8):
                        last = mm(PS(1024 + S * d, S), ring[:, r % RING, P * d:P * d + P], CF[:, b, :],
                                  start=(first and d % 2 == 0), stop=False, skip_group_check=True)
                        if d == 0:
                            last.then_inc(sem("slot_begun"), 1)
                    last.then_inc(sem("coef_used"), 1)

                up(0, 0, w0, lambda: arrived(w0), True)
                up(1, 1, w0 + 1, lambda: arrived(w0 + 1), True)
                down(0, 0, w0 + 2, lambda: arrived(w0 + 2), True)
                w1 = w0 + 3
                with pe.Fori(0, (NEXP - 2) // 2) as i:
                    def arrived_in_loop(w):
                        pe.wait_ge(sem(f"slot_loaded{w % RING}"), i * 16 + 16 * (w // RING + 1))

                    for b in range(2):
                        w = w1 + 2 * b
                        up(i * 2 + (b + 2), b, w, lambda: arrived_in_loop(w))
                        down(i * 2 + (b + 1), 1 - b, w + 1, lambda: arrived_in_loop(w + 1))
                w = w1 + 2 * (NEXP - 2)
                down(NEXP - 1, 1, w, lambda: arrived(w))
                L.slots = w + 1
                L.take("acc_evacuated")

            rowsum(SQX2, 8, 512)
            L.take("normed")
            linear(16, 8, H, 512)
            evacuated()
            rowsum(Z[:, 8:16, :], 8, 512, None)
            rowsum(SQZ, 8, 512)
            L.take("v_normed")
            for h in range(8):
                for n in range(4):
                    last = pe.transpose(PS(P * (4 * h + n), P), Z[:, 8 + h, P * n:P * n + P], ident)
            L.mark(last, "v_turned")
            L.take("v_turned_evacuated")
            arrived(L.slots)
            pe.wait_ge(sem("bs_loaded"), 16)
            for h in range(8):
                for n in range(4):
                    o = PS(P * (4 * h + n), P)
                    last = mm(o, ZT[:, 4 * h + n, :], ring[:, L.slots % RING, P * h:P * h + P], start=(n == 0),
                              stop=False, skip_group_check=True)
                    if h == 0 and n == 0:
                        last.then_inc(sem("slot_begun"), 1)
                    last = mm(o, ones[0:1, :], BS[:, P * h:P * h + P], start=False, stop=True,
                              skip_group_check=True)
            L.slots += 1
            L.mark(last, "mixed")
            L.take("mixed_used")
            linear(8, 8, Z, 512)
            rowsum(SQX2, 8, 512)
            L.take("normed")
            peer(0, 0)
            peer(1, S)
            rowsum(SQX2, 8, 512)
            L.take("normed")
            linear(8, 8, H, 512)
            evacuated()
            for q in range(2):
                if q:
                    L.take("tokens_evacuated")
                for d in range(4):
                    for s in range(8):
                        last = pe.transpose(PS(P * (8 * d + s), P, parts=64),
                                            UT[:, 4 * q + d, s:512:8], ident)
                L.mark(last, "tokens_turned")
            L.take("tokens_evacuated")
            for g in range(NG):
                last = pe.transpose(PS(64 * g, 64), UN[:, g, :, :].rearrange("p s c -> p (s c)"), ident[0:64, 0:64])
            L.mark(last, "groups_turned")
            L.take("groups_ready")

            def inject(g, first):
                pe.wait_ge(sem("inj_ready"), g + 1)
                for r in range(2):
                    last = pe.transpose(bank(0)[:, P * r:P * r + P], WC[:, r, :], ident)
                last.then_inc(sem("inj_turned"), 1)
                pe.wait_ge(sem("inj_evacuated"), g + 1)
                if not first:
                    pe.wait_ge(sem("injected_evacuated"), g)
                for r in range(2):
                    last = mm(bank(1)[:, 64 * r:64 * r + 64], STG[:, r, :], UG[:, g, :], start=(r == 0), stop=True,
                              skip_group_check=True)
                last.then_inc(sem("injected"), 1)

            inject(0, True)
            with pe.Fori(1, NG) as g:
                inject(g, False)

            def readout(g, first):
                pe.wait_ge(sem("toeplitz_ready"), g + 1)
                if not first:
                    pe.wait_ge(sem("toeplitz_evacuated"), g)
                for t in range(8):
                    for r in range(2):
                        last = mm(bank(0)[:, 16 * t:16 * t + 16], WW[:, r, 16 * (7 - t):16 * (7 - t) + P],
                                  CC[:, 2 * r, g, :], start=(t == 0 and r == 0), stop=(r == 1),
                                  skip_group_check=True)
                last.then_inc(sem("toeplitz"), 1)
                pe.wait_ge(sem("toeplitz_evacuated"), g + 1)
                pe.wait_ge(sem("readout_ready"), g + 1)
                if not first:
                    pe.wait_ge(sem("y_evacuated"), g)
                o = bank(1)[0:NCH, 0:P]
                mm(o, STU[:, 0, :], STG[:, 0, :], start=True, stop=False)
                mm(o, STU[:, 1, :], WC[:, 0, :], start=False, stop=False)
                mm(o, STU[:, 2, :], WC[:, 1, :], start=False, stop=True).then_inc(sem("y_ready"), 1)

            readout(0, True)
            with pe.Fori(1, NG) as g:
                readout(g, False)
            pe.wait_ge(sem("y_evacuated"), NG)
            for d in range(8):
                for s in range(8):
                    last = pe.transpose(PS(NCH * (8 * d + s), NCH), YN[:, s, P * d:P * d + P],
                                        ident[0:NCH, 0:NCH])
            L.mark(last, "y_turned")
            L.take("y_gelu")
            linear(8, 8, YT, S)
            linear(8, 8, YT, S)
            rowsum(SQX2, 8, S)
            L.take("normed")
            peer(2, 0)
            rowsum(SQX, 8, S)
            assert L.slots == SLOTS_READ

        @block.scalar
        def _(act):
            L = Line(act, sem, sem("act_chain"))
            f = act.activation
            copy = lambda o, i: f(o, i, ACT.Copy)

            def evacuate(tiles, fn):
                l0 = L.lin
                turns = L.loop(tiles // 2, 0) if tiles >= 8 else [0]
                for i in turns:
                    for b in range(2):
                        act.wait_ge(sem("lin_ready"), i * 2 + (l0 + b + 1))
                        fn(i * 2 + b, bank(b)).then_inc(sem("lin_free"), 1)
                act.wait_ge(sem("lin_free"), l0 + tiles)
                L.lin += tiles

            def others(tiles):
                L.lin += tiles

            def norm(src, dst, ready):
                if ready:
                    L.take(ready)
                L.give(f(dst, src, ACT.Square), "squares")
                root(R1[:, 0:src.shape[2]], R2[:, 0:src.shape[2]])

            def root(a, b):
                L.take("var")
                L.give(f(b, a, ACT.Sqrt), "rstd")

            act.wait_ge(sem("inputs_loaded"), 64)
            L.give(f(CS, col("cond", 0, 16).rearrange("p (a b) -> p a b", b=2), ACT.Silu), "cond_silu")
            norm(X[:, :, 0:S], SQX, None)
            others(24)
            evacuate(8, lambda t, ps: f(GT[:, t, :], ps[:, 0:S], ACT.Silu))
            others(8)
            evacuate(16, lambda t, ps: f(GB[:, t, :], ps[:, 0:S], ACT.Sigmoid))
            act.wait_ge(sem("lin_free"), L.lin)
            a = AB[0:8, :]
            L.do(f(ROWS[:, 0, :], AB[32:40, :], ACT.Sigmoid))
            L.do(f(QKV, QKV, ACT.Silu))
            L.give(f(SQ, QKV[:, 0:16, :], ACT.Square), "head_squares")
            L.do(f(a, a, ACT.Identity, bias=col("dt_bias")[0:8, :]))
            L.do(f(ROWS[:, 3, :], a, ACT.Abs))
            L.do(f(ROWS[:, 3, :], ROWS[:, 3, :], ACT.Exp, scale=-1.0))
            L.do(f(ROWS[:, 3, :], ROWS[:, 3, :], ACT.Ln, bias=1.0))
            L.give(f(TSUM[0:8, 0:1], col("a_log")[0:8, :], ACT.Exp), "softplus_parts")
            L.take("decay_rows")
            L.do(f(ROWS[:, 2, :], ROWS[:, 1, :], ACT.Exp))
            L.give(f(ROWS[:, 3, :], ROWS[:, 3, :], ACT.Exp), "row_exps")
            L.take("head_var")
            L.give(f(SQ, SQ, ACT.Sqrt), "head_rstd")
            L.take("rows_spread")
            L.give(copy(BETA, PS(0, 8, S)), "beta_evacuated")
            L.take("exps_spread")
            L.do(copy(EGB, PS(0, 8, P)))
            L.give(copy(EDB, PS(1024, 8, P)), "exps_evacuated")
            L.take("decay_args")
            L.give(f(DEC, DEC, ACT.Exp), "decay_exp")
            L.take("vt_ready")
            L.do(copy(VT, PS(0, 16, P)))
            L.give(copy(KDC, PS(2048, 8, P)), "vt_evacuated")
            L.take("gdn_out")
            L.give(f(SQO, OG, ACT.Square), "squares")
            root(RSO, RSO)
            others(8)
            act.wait_ge(sem("lin_free"), L.lin)
            L.give(f(SQM, CQ, ACT.Square), "squares")
            root(R1[:, 0:S], R2[:, 0:S])
            L.take("latent_q_normed")
            L.give(f(SQM[:, 0:2, :], CKV, ACT.Square), "squares")
            root(R1[:, 0:S], R2[:, 0:S])
            evacuate(8, lambda t, ps: copy(QN[:, t, :], ps[:, 0:S]))
            others(8)
            evacuate(8, lambda t, ps: copy(KN[:, t, :], ps[:, 0:S]))
            L.take("v_ready")
            L.give(copy(VM, PS(1024, 2, D)), "v_evacuated")
            L.take("scores_shifted")
            L.give(f(SC, SC, ACT.Exp), "probs_exp")
            L.take("probs_turned")
            L.give(copy(PT, PS(0, 8, 512)[:, :, 0:384]), "probs_evacuated")
            others(16)
            act.wait_ge(sem("lin_free"), L.lin)
            norm(X[:, :, 0:S], SQX, None)
            others(FT)
            act.wait_ge(sem("lin_free"), L.lin)
            L.give(f(UF[:, 0:FK, :], UF[:, 0:FK, :], ACT.Silu), "ffn_gate")
            others(8)
            act.wait_ge(sem("lin_free"), L.lin)
            norm(X[:, :, 0:S], SQX, None)

            def peer(p, off):
                evacuate(32, lambda t, ps: copy(QT[:, t, :], ps[:, 0:S]))
                L.take("gate_args")
                L.give(f(TS, TS, ACT.Exp), "gate_exp")

                def gates(n, b, t0):
                    act.wait_ge(sem("gates_built"), n + 1)
                    copy(G[:, :, bass.ds(t0, 8)], PS(1024 * b, 8, P).rearrange("p t j -> p j t"))\
                        .then_inc(sem("gates_evacuated"), 1)

                with act.Fori(0, 16) as i:
                    for b in range(2):
                        gates(i * 2 + (32 * p + b), b, i * 16 + 8 * b)

                n0 = NEXP * p

                def gelu(j, b, first):
                    act.wait_ge(sem("up_ready"), j + (n0 + 1))
                    if not first:
                        act.wait_ge(sem("coef_ready"), j + (n0 - 1))
                    f(AC[:, b, :], bank(b)[:, 0:S], ACT.Gelu_apprx_tanh).then_inc(sem("gelu_done"), 1)

                gelu(0, 0, True)
                gelu(1, 1, True)
                with act.Fori(1, NEXP // 2) as i:
                    for b in range(2):
                        gelu(i * 2 + b, b, False)
                L.take("acc_evacuated")

            L.take("mods_used")
            norm(X, SQX2, None)
            evacuate(16, lambda t, ps: f(Z[:, t, :], ps, ACT.Gelu_apprx_tanh))
            L.take("centered")
            L.give(f(SQZ, Z[:, 8:16, :], ACT.Square), "squares")
            root(R1, R2)
            others(8)
            act.wait_ge(sem("lin_free"), L.lin)
            norm(X, SQX2, None)
            peer(0, 0)
            peer(1, S)
            norm(X, SQX2, None)
            act.wait_ge(sem("ssm_loaded"), 48)
            L.give(f(TP[:, 0, :], LAM[:, 2, :], ACT.Exp), "ssm_step")
            L.take("ssm_angle")
            L.do(f(TP[:, 6, :], TP[:, 1, :], ACT.Exp))
            L.do(f(TP[:, 7, :], TP[:, 4, :], ACT.Sin))
            L.give(f(TP[:, 8, :], TP[:, 5, :], ACT.Sin), "ssm_trig")
            evacuate(8, lambda t, ps: copy(UT[:, t, :], ps))
            for q in range(2):
                L.take("tokens_turned")
                for d in range(4):
                    last = copy(UN[:, 8 * (4 * q + d):8 * (4 * q + d) + 8, :, :].rearrange("p g s c -> p s g c"),
                                PS(1024 * d, 8, 8, 16, parts=64))
                L.give(last, "tokens_evacuated")
            L.take("groups_turned")
            L.give(copy(UG, PS(0, NG, 64)), "groups_ready")
            with act.Fori(0, NG) as g:
                act.wait_ge(sem("inj_turned"), g + 1)
                copy(STG, bank(0)[:, 0:2 * P].rearrange("p (r m) -> p r m", r=2)).then_inc(sem("inj_evacuated"), 1)
                act.wait_ge(sem("injected"), g + 1)
                copy(XS[:, :, :, g], bank(1)[:, 0:P].rearrange("p (r n) -> p n r", r=2))\
                    .then_inc(sem("injected_evacuated"), 1)
            L.take("scanned")
            with act.Fori(0, NG) as g:
                act.wait_ge(sem("toeplitz"), g + 1)
                copy(STU[:, 0, :], UG[:, g, 0:NCH])
                copy(STU[:, 1:3, :], HS[:, :, :, g].rearrange("p n r -> p r n"))
                copy(STG[:, 0, :], bank(0)[:, 0:P]).then_inc(sem("toeplitz_evacuated"), 1)
                act.wait_ge(sem("y_ready"), g + 1)
                copy(YN[:, :, bass.ds(g * 16, 16)], bank(1)[0:NCH, 0:P].rearrange("p (s c) -> p s c", s=8))\
                    .then_inc(sem("y_evacuated"), 1)
            L.take("y_summed")
            L.give(f(YT, YT, ACT.Gelu_apprx_tanh), "y_gelu")
            evacuate(8, lambda t, ps: f(SG[:, t, :], ps[:, 0:S], ACT.Sigmoid))
            others(8)
            act.wait_ge(sem("lin_free"), L.lin)
            norm(X[:, :, 0:S], SQX2[:, :, 0:S], None)
            peer(2, 0)
            norm(X[:, :, 0:S], SQX, None)

        @block.vector
        def _(dve):
            L = Line(dve, sem, sem("dve_chain"))
            tt, ts, stt, cp = dve.tensor_tensor, dve.tensor_scalar, dve.scalar_tensor_tensor, dve.tensor_copy

            def over(a, n, at):
                a = a.unsqueeze(at)
                shape = list(a.shape)
                shape[at] = n
                return a.to_broadcast(shape)

            def evacuate(tiles, fn, per):
                l0 = L.lin
                turns = L.loop(tiles // 2, 2 * per) if tiles >= 8 else [0]
                for i in turns:
                    for b in range(2):
                        dve.wait_ge(sem("lin_ready"), i * 2 + (l0 + b + 1))
                        fn(i * 2 + b, bank(b), b).then_inc(sem("lin_free"), 1)
                dve.wait_ge(sem("lin_free"), l0 + tiles)
                L.lin += tiles

            def others(tiles):
                L.lin += tiles

            def inv_var(scale, src, dst):
                L.take("rowsum")
                L.do(ts(dst, src, scale, EPS, ALU.mult, ALU.add))
                L.give(dve.reciprocal(dst, dst), "var")
                L.take("rstd")

            def norm(src, g, dst, kt, inv, n=S):
                inv_var(inv, bank(7)[:, 0:n], R1[:, 0:n])
                for k in range(kt):
                    last = stt(dst[:, k, :], src[:, k, :], g[:, k:k + 1], R2[:, 0:n], ALU.mult, ALU.mult)
                return last

            def scalar_of(name, t, k=0, per=1):
                return small[:, bass.ds(t * per + (COLS[name][0] + k), 1)]

            def conv(taps, name, dst):
                def fn(t, ps, b):
                    w = lambda j: scalar_of(name, t, j, taps)
                    L.do(ts(dst[:, t, :], ps[:, 0:S], w(taps - 1), None, ALU.mult))
                    for j in range(1, taps):
                        ins = stt(dst[:, t, j:S], ps[:, 0:S - j], w(taps - 1 - j), dst[:, t, j:S],
                                  ALU.mult, ALU.add)
                        if j < taps - 1:
                            L.do(ins)
                    return ins
                return fn

            dve.wait_ge(sem("inputs_loaded"), 64)
            L.give(norm(X[:, :, 0:S], col("norm_mix", 0, 8), H[:, :, 0:S], 8, 1.0 / D), "normed")
            evacuate(24, conv(4, "conv", QKV), 3)
            others(8)
            evacuate(8, lambda t, ps, b: cp(MISC[:, t, :], ps[:, 0:S]), 0)
            others(16)
            L.take("softplus_parts")
            L.do(stt(ROWS[:, 3, :], AB[0:8, :], 0.0, ROWS[:, 3, :], ALU.max, ALU.add))
            L.do(ts(ROWS[:, 3, :], ROWS[:, 3, :], TSUM[0:8, 0:1], -1.0, ALU.mult, ALU.mult))
            for c in range(2):
                t = slice(P * c, P * c + P)
                L.do(dve.tensor_tensor_scan(ROWS[:, 1, t], ones[0:8, :], ROWS[:, 3, t], 0.0, ALU.mult, ALU.add))
            for c in range(2):
                t = slice(P * c, P * c + P)
                ins = ts(ROWS[:, 3, t], ROWS[:, 1, t], -1.0, ROWS[:, 1, P * c + P - 1:P * c + P],
                         ALU.mult, ALU.add)
            L.give(ins, "decay_rows")
            L.take("head_sums")
            L.give(ts(SQ, PS(0, 16, S), EPS, None, ALU.add), "head_sums_used")
            L.give(dve.reciprocal(SQ, SQ), "head_var")
            L.take("head_rstd")
            stt(Q_, Q_, float(P) ** -0.5, SQ[:, 0:8, :], ALU.mult, ALU.mult)
            L.do(tt(K_, K_, SQ[:, 8:16, :], ALU.mult))
            L.take("rows_spread")
            L.give(cp(DEC, PS(2048, 8, S)), "decay_evacuated")
            L.take("exps_spread")
            L.do(ts(NGC, PS(2048, 2, 8), -1.0, None, ALU.mult))
            for h in range(NH):
                for c in range(2):
                    d = DEC[:, h, P * c:P * c + P]
                    ins = ts(d, d, NGC[:, c, h:h + 1], 0.0, ALU.add, ALU.min)
            L.give(ins, "decay_args")
            L.take("beta_evacuated")
            L.take("exps_evacuated")
            L.do(tt(V_, V_, BETA, ALU.mult))
            L.do(tt(KDC, K_[:, :, 0:P], EDB, ALU.mult))
            L.do(tt(QD, Q_[:, :, P:S], EGB, ALU.mult))
            L.do(tt(KBG, K_[:, :, P:S], BETA[:, :, P:S], ALU.mult))
            L.give(tt(KBG, KBG, EGB, ALU.mult), "gdn_operands")
            L.take("decay_exp")
            dec = DEC.rearrange("p h (c i) -> p (h c) i", c=2)
            L.do(tt(dec, dec, over(col1("causal"), 16, 1), ALU.mult))
            L.take("kk_ready")
            L.do(tt(LT, PS(0, 16, P), BETA.rearrange("p h (c i) -> p (h c) i", c=2), ALU.mult))
            L.do(tt(LT, LT, dec, ALU.mult))
            L.give(tt(AT, PS(2048, 16, P), dec, ALU.mult), "kk_evacuated")
            levels = col1("levels", LEVELS, P)
            L.do(tt(ML, LT, over(levels[:, 0, :], 16, 1), ALU.mult))
            L.give(stt(TT, ML, -1.0, over(ident, 16, 1), ALU.mult, ALU.add), "inverse_begun")
            L.take("inverse_turned")
            L.do(cp(TI, PS(0, 16, P)))
            for lev in range(1, LEVELS):
                L.give(tt(ML, LT, over(levels[:, lev, :], 16, 1), ALU.mult), "level_masked")
                L.take("level_inner")
                L.give(cp(AM, PS(0, 16, P)), "level_inner_evacuated")
                L.take("level_outer")
                L.do(tt(TT, TT, PS(0, 16, P), ALU.subtract))
                if lev < LEVELS - 1:
                    L.do(tt(TI, TI, PS(2048, 16, P), ALU.subtract))
            L.give(cp(TMAX, ident[:, 0:16]), "inverse_ready")
            L.take("new0_ready")
            L.give(cp(VN0, PS(0, 8, P)), "new0_evacuated")
            L.take("state_ready")
            L.do(cp(OG[:, :, 0:P], PS(2048, 8, P)))
            L.give(cp(S1, PS(1024, 8, P)), "state_evacuated")
            L.take("old_value_ready")
            L.give(tt(RR, VT.rearrange("p (h c) d -> p h c d", c=2)[:, :, 1, :], PS(0, 8, P), ALU.subtract),
                   "residual_ready")
            L.take("new1_ready")
            L.give(cp(VN1, PS(1024, 8, P)), "new1_evacuated")
            L.take("gdn_out1")
            L.give(cp(OG[:, :, P:S], PS(3072, 8, P)), "gdn_out")
            inv_var(1.0 / P, PS(0, 8, S), RSO)
            L.do(stt(OG, OG, col("gdn_norm"), RSO, ALU.mult, ALU.mult))
            L.give(tt(OG, OG, GT, ALU.mult), "gdn_gated")
            evacuate(8, lambda t, ps, b: tt(YA[:, t, :], ps[:, 0:S], GB[:, t, :], ALU.mult), 0)
            L.give(norm(CQ, col("q_norm", 0, 3), CQ, 3, 1.0 / 384), "latent_q_normed")
            L.give(norm(CKV, col("kv_norm", 0, 2), CKV, 2, 1.0 / 256), "latent_normed")
            others(8)
            evacuate(8, lambda t, ps, b: cp(QPR[:, t, :], ps[:, 0:S]), 0)
            cos, sin = col1("cos"), col1("sin")
            L.do(tt(TMP, QP, over(cos, 4, 1), ALU.mult))
            L.do(tt(QPS, QPS, over(sin, 4, 1), ALU.mult))
            L.do(tt(QP, TMP, QPS, ALU.add))
            L.do(tt(KP, KP, cos, ALU.mult))
            L.do(tt(KPS, KPS, sin, ALU.mult))
            L.do(dve.memset(KPP, 0.0))
            tt(KPP[0:64, 0, :], KP[0:64, :], KPS[0:64, :], ALU.add)
            L.give(tt(KPP[64:P, 1, :], KP[64:P, :], KPS[64:P, :], ALU.add), "rope_ready")
            others(8)
            L.take("scores_ready")
            sc = PS(0, 8, 512)
            scale = float(P + 64) ** -0.5
            neg = over(col1("neg"), 8, 1)
            stt(SC[:, :, 0:P], sc[:, :, 0:P], scale, neg, ALU.mult, ALU.add)
            ts(SC[:, :, P:S], sc[:, :, P:S], scale, None, ALU.mult)
            L.do(stt(SC[:, :, S:384], sc[:, :, S:384], scale, neg, ALU.mult, ALU.add))
            parts = ((slice(0, P), 0, P), (slice(P, 384), 8, S))
            for s, o, n in parts:
                L.do(dve.tensor_reduce(TMAX[:, o:o + 8], SC[:, :, s], AX, ALU.max))
            for s, o, n in parts:
                ins = tt(SC[:, :, s], SC[:, :, s], over(TMAX[:, o:o + 8], n, 2), ALU.subtract)
            L.give(ins, "scores_shifted")
            L.take("probs_exp")
            for s, o, n in parts:
                L.do(dve.tensor_reduce(TSUM[:, o:o + 8], SC[:, :, s], AX, ALU.add))
            L.do(dve.reciprocal(TSUM, TSUM))
            for s, o, n in parts:
                ins = tt(SC[:, :, s], SC[:, :, s], over(TSUM[:, o:o + 8], n, 2), ALU.mult)
            L.give(ins, "probs_ready")
            L.take("attention_out")
            L.give(cp(OB, PS(0, 8, S)), "attention_ready")

            def merge(t, ps, b):
                L.do(tt(TME[:, b, :], ps[:, 0:S], GB[:, t + 8, :], ALU.mult))
                return tt(MG[:, t, :], TME[:, b, :], YA[:, t, :], ALU.add)

            evacuate(8, merge, 1)
            add_x = lambda t, ps, b: tt(X[:, t, 0:S], ps[:, 0:S], X[:, t, 0:S], ALU.add)
            evacuate(8, add_x, 0)
            L.give(norm(X[:, :, 0:S], col("norm_ffn", 0, 8), H[:, :, 0:S], 8, 1.0 / D), "normed")
            evacuate(FT, conv(3, "conv_ffn", UF), 2)
            L.take("ffn_gate")
            L.give(tt(UF[:, 0:FK, :], UF[:, 0:FK, :], UF[:, FK:FT, :], ALU.mult), "ffn_inner")
            evacuate(8, add_x, 0)
            L.do(norm(X[:, :, 0:S], col("norm_final", 0, 8), X[:, :, 0:S], 8, 1.0 / D))
            dve.wait_ge(sem("pos_loaded"), 16)
            L.give(tt(X[:, :, 0:S], X[:, :, 0:S], H[:, :, S:2 * S], ALU.add), "x_normed")
            L.take("mods_ready")
            mod = MOD.rearrange("p l t c -> p (l t) c")
            L.give(tt(mod, PS(3072, 96, 2), over(col("ada_b", 0, 96), 2, 2), ALU.add), "bs_room")
            for l in range(2):
                for w in range(2):
                    g = over(col("norm2" if w else "norm1", 8 * l, 8), 2, 2)
                    ins = stt(SA[:, l, w], MOD[:, l, 24 * w + 8:24 * w + 16, :], 1.0, g, ALU.add, ALU.mult)
            L.give(ins, "mods_used")

            def modulated(l, w, halves):
                n = S * halves
                inv_var(1.0 / D, bank(7)[:, 0:n], R1[:, 0:n])
                L.do(tt(H[:, :, 0:n], X[:, :, 0:n], over(R2[:, 0:n], 8, 1), ALU.mult))
                for c in range(halves):
                    for k in range(8):
                        h = H[:, k, S * c:S * c + S]
                        ins = ts(h, h, SA[:, l, w, k, c:c + 1], MOD[:, l, 24 * w + k, c:c + 1], ALU.mult, ALU.add)
                L.give(ins, "normed")

            def top16(val, idx, src, wk):
                L.do(dve.max(val[:, 0:8], src))
                L.do(dve.max_index(idx[:, 0:8], val[:, 0:8], src))
                L.do(dve.match_replace(wk, val[:, 0:8], src, LOWEST))
                L.do(dve.max(val[:, 8:16], wk))
                L.do(dve.max_index(idx[:, 8:16], val[:, 8:16], wk))

            def peer(p, l, off, c):
                others(32)
                L.take("key_scores")
                L.do(cp(SCO, PS(0, 2, 16, P)))
                for i in range(2):
                    for hk in range(16):
                        top16(SV[:, i, hk, :], IDX[:, i, hk, :], SCO[:, i, hk, :], WK[:, 0:P])
                sv = SV.rearrange("p i (h k) a -> p (i h) k a", k=2)
                cand = CAND.rearrange("p h (a b) -> p h a b", a=16)
                L.do(tt(cand, over(sv[:, :, 0, :], 16, 3), over(sv[:, :, 1, :], 16, 2), ALU.add))
                for ih in range(16):
                    top16(TS[:, ih, :], TC[:, ih, :], CAND[:, ih, :], WK)
                tc = TC.rearrange("p h k -> p (h k)")
                L.do(ts(CI[:, 0, :], tc, 4, None, ALU.logical_shift_right))
                L.do(ts(CI[:, 1, :], tc, 15, None, ALU.bitwise_and))
                L.do(cp(CF_, CI))
                L.do(cp(IDF, IDX))
                idf = IDF.rearrange("p i (h k) a -> p (i h) k a", k=2)
                oh = OH.rearrange("p (h k) a -> p h k a", h=16)
                for m in range(2):
                    L.do(tt(OH, over(CF_[:, m, :], 16, 2), over(iota[:, 0:16], 256, 1), ALU.is_equal))
                    L.do(tt(oh, oh, over(idf[:, :, m, :], 16, 2), ALU.mult))
                    L.do(dve.tensor_reduce(KK[:, m, :], OH, AX, ALU.add))
                L.do(tt(oh[:, 0, :, :], TS, over(TS[:, :, 0], 16, 2), ALU.subtract))
                L.give(cp(TS, oh[:, 0, :, :]), "gate_args")
                L.take("gate_exp")
                L.do(dve.tensor_reduce(TSUM, TS, AX, ALU.add))
                L.do(dve.reciprocal(TSUM, TSUM))
                L.give(tt(KK[:, 2, :].rearrange("p (h k) -> p h k", h=16), TS, over(TSUM, 16, 2), ALU.mult),
                       "chosen")
                L.take("chosen_turned")
                L.give(cp(K3, PS(0, 3, S)), "chosen_evacuated")

                start, per = L.k, 1

                def onehots(n, b, t0, first):
                    if not first:
                        dve.wait_ge(sem("gates_built"), n - 1)
                    k = lambda m: over(K3[:, m, bass.ds(t0, 8)], P, 2)
                    it = over(iota, 8, 1)
                    L.do(tt(EA[:, b], k(0), it, ALU.is_equal))
                    L.do(tt(EA[:, b], EA[:, b], k(2), ALU.mult))
                    tt(EB[:, b], k(1), it, ALU.is_equal).then_inc(sem("onehots_ready"), 1)

                for b in range(2):
                    onehots(32 * p + b, b, 8 * b, True)
                for i in L.loop(15, 4):
                    for b in range(2):
                        onehots(i * 2 + (32 * p + 2 + b), b, i * 16 + (16 + 8 * b), False)

                n0 = NEXP * p

                def coef(j, b, first):
                    dve.wait_ge(sem("gelu_done"), j + (n0 + 1))
                    if not first:
                        dve.wait_ge(sem("coef_used"), j + (n0 - 1))
                    tt(CF[:, b, :], AC[:, b, :], G[:, j, :], ALU.mult).then_inc(sem("coef_ready"), 1)

                dve.wait_ge(sem("gates_evacuated"), 32 * p + 32)
                coef(0, 0, True)
                coef(1, 1, True)
                with dve.Fori(1, NEXP // 2) as i:
                    for b in range(2):
                        coef(i * 2 + b, b, False)
                dve.wait_ge(sem("coef_used"), NEXP * p + NEXP)
                for d in range(8):
                    x = X[:, d, off:off + S]
                    ins = stt(x, PS(1024 + S * d, S), MOD[:, l, 40 + d, c:c + 1], x, ALU.mult, ALU.add)
                L.give(ins, "acc_evacuated")

            modulated(0, 0, 2)
            others(16)
            L.take("rowsum")
            L.do(ts(R1, bank(7), 1.0 / D, None, ALU.mult))
            zv = Z[:, 8:16, :]
            L.give(tt(zv, zv, over(R1, 8, 1), ALU.subtract), "centered")
            inv_var(1.0 / D, bank(7), R1)
            L.do(tt(zv, zv, over(R2, 8, 1), ALU.mult))
            for k in range(8):
                ins = ts(zv[:, k, :], zv[:, k, :], col("ln_g", k), col("ln_b", k), ALU.mult, ALU.add)
            L.give(ins, "v_normed")
            L.take("v_turned")
            L.give(cp(ZT, PS(0, 32, P)), "v_turned_evacuated")
            L.take("mixed")
            L.give(tt(Z[:, 0:8, :], Z[:, 0:8, :], PS(0, 8, 512), ALU.mult), "mixed_used")

            def add_gated(t, ps, b):
                for c in range(2):
                    x = X[:, t, S * c:S * c + S]
                    g = small[:, bass.ds(t * 2 + (T0 + 2 * 16 + c), 1)]
                    ins = stt(x, ps[:, S * c:S * c + S], g, x, ALU.mult, ALU.add)
                return ins

            evacuate(8, add_gated, 0)
            modulated(0, 1, 2)
            peer(0, 0, 0, 0)
            peer(1, 0, S, 1)
            L.give(cp(TMAX, ident[:, 0:16]), "ssm_room")
            modulated(1, 0, 2)
            others(8)
            T = lambda k: TP[:, k, :]
            lr, li = LAM[:, 0, :], LAM[:, 1, :]
            L.take("ssm_step")
            L.do(tt(T(1), lr, T(0), ALU.mult))
            L.do(tt(T(2), li, T(0), ALU.mult))
            L.do(ts(T(3), T(2), 1.0 / TWO_PI, None, ALU.mult))
            L.do(ts(T(3), T(3), MAGIC, None, ALU.add))
            L.do(ts(T(3), T(3), MAGIC, None, ALU.subtract))
            L.do(stt(T(4), T(3), -C1, T(2), ALU.mult, ALU.add))
            L.do(stt(T(4), T(3), -C2, T(4), ALU.mult, ALU.add))
            L.do(stt(T(4), T(3), -C3, T(4), ALU.mult, ALU.add))
            L.do(ts(T(4), T(4), 3.1415925, -3.1415925, ALU.min, ALU.max))
            L.give(ts(T(5), T(4), 0.5, None, ALU.mult), "ssm_angle")
            L.take("ssm_trig")
            L.do(tt(T(9), T(8), T(8), ALU.mult))
            L.do(ts(T(9), T(9), -2.0, 1.0, ALU.mult, ALU.add))
            ar, ai = PW[:, 1, 0, :], PW[:, 1, 1, :]
            L.do(tt(ar, T(6), T(9), ALU.mult))
            L.do(tt(ai, T(6), T(7), ALU.mult))
            L.do(tt(T(10), lr, lr, ALU.mult))
            L.do(tt(T(11), li, li, ALU.mult))
            L.do(tt(T(10), T(10), T(11), ALU.add))
            L.do(dve.reciprocal(T(10), T(10)))
            L.do(ts(T(11), ar, -1.0, None, ALU.add))

            def cross(out, a, b, c, d, op, t1, t2):
                tt(t1, a, b, ALU.mult)
                L.do(tt(t2, c, d, ALU.mult))
                L.do(tt(out, t1, t2, op))

            cross(T(14), T(11), lr, ai, li, ALU.add, T(12), T(13))
            L.do(tt(T(14), T(14), T(10), ALU.mult))
            cross(T(15), ai, lr, T(11), li, ALU.subtract, T(12), T(13))
            L.do(tt(T(15), T(15), T(10), ALU.mult))
            cr, ci = over(T(14), 16, 2), over(T(15), 16, 2)
            cross(BB[:, 0], RAW[:, 0], cr, RAW[:, 1], ci, ALU.subtract, TB1, TB2)
            cross(BB[:, 1], RAW[:, 1], cr, RAW[:, 0], ci, ALU.add, TB1, TB2)
            dve.memset(PW[:, 0, 0, :], 1.0)
            dve.memset(PW[:, 0, 1, :], 0.0)
            L.do(ts(CC[:, 2], CC[:, 1], -1.0, None, ALU.mult))
            for j in range(2, 9):
                cross(PW[:, j, 0, :], PW[:, j - 1, 0, :], ar, PW[:, j - 1, 1, :], ai, ALU.subtract, T(12), T(13))
                cross(PW[:, j, 1, :], PW[:, j - 1, 0, :], ai, PW[:, j - 1, 1, :], ar, ALU.add, T(12), T(13))
            L.do(dve.memset(PWM, 0.0))
            F, B = slice(0, 64), slice(64, P)
            for m in range(8):
                cp(PWM[F, :, :, m], PW[F, 7 - m, :, :])
                cp(PWM[B, :, :, m + 7], PW[B, m, :, :])
                cp(PWI[F, :, :, m], PW[F, 7 - m, :, :])
                cp(PWI[B, :, :, m], PW[B, m, :, :])
                cp(PWO[F, :, :, m], PW[F, m + 1, :, :])
                cp(PWO[B, :, :, m], PW[B, 8 - m, :, :])
            for r in range(2):
                cp(A1C[:, r, :], PW[:, 8, 0, :])
            ts(A2C[:, 0, :], PW[:, 8, 1, :], -1.0, None, ALU.mult)
            L.do(cp(A2C[:, 1, :], PW[:, 8, 1, :]))

            def outer(out, pw, g, mat, n, re_im):
                a = [over(pw[:, r, g, :], 16, 2) for r in range(2)]
                m = [over(mat[:, r, g, :], n, 1) for r in range(3 if mat.shape[1] == 3 else 2)]
                t1 = WT1[:, 0:16 * n].rearrange("p (n c) -> p n c", c=16)
                t2 = WT2[:, 0:16 * n].rearrange("p (n c) -> p n c", c=16)
                (p1, m1), (p2, m2), op = re_im
                tt(t1, a[p1], m[m1], ALU.mult)
                L.do(tt(t2, a[p2], m[m2], ALU.mult))
                return tt(out.rearrange("p (n c) -> p n c", c=16), t1, t2, op)

            RE, IM = ((0, 0), (1, 1), ALU.subtract), ((0, 1), (1, 0), ALU.add)

            def injection(g):
                L.do(outer(WC[:, 0, :], PWI, g, BB, 8, RE))
                outer(WC[:, 1, :], PWI, g, BB, 8, IM).then_inc(sem("inj_ready"), 1)

            injection(0)
            for i in L.loop(NG - 1, 3):
                dve.wait_ge(sem("inj_ready"), i + 1)
                dve.wait_ge(sem("inj_turned"), i + 1)
                injection(i + 1)
            dve.wait_ge(sem("injected_evacuated"), NG)
            h = HST[:, 0]
            L.do(dve.memset(h, 0.0))

            def step(fwd, bwd):
                tt(ST1, A1C, h, ALU.mult)
                tt(ST2[:, 0, :], A2C[:, 0, :], h[:, 1, :], ALU.mult)
                L.do(tt(ST2[:, 1, :], A2C[:, 1, :], h[:, 0, :], ALU.mult))
                L.do(tt(ST1, ST1, ST2, ALU.add))
                tt(h[F], ST1[F], XS[F, fwd], ALU.add)
                L.do(tt(h[B], ST1[B], XS[B, bwd], ALU.add))

            for i in L.loop(NCH, 3):
                step(i + NCH, i * -1 + (2 * NCH - 1))
            for i in L.loop(NCH, 4):
                cp(HS[F, i], h[F])
                L.do(cp(HS[B, i * -1 + (NCH - 1)], h[B]))
                step(i, i * -1 + (NCH - 1))
            L.give(cp(TMAX, ident[:, 0:16]), "scanned")

            def outputs(g, first):
                if not first:
                    dve.wait_ge(sem("toeplitz"), g)
                L.do(outer(WW[:, 0, :], PWM, g, BB, 15, RE))
                last = outer(WW[:, 1, :], PWM, g, BB, 15, IM)
                last.then_inc(sem("toeplitz_ready"), 1)
                dve.wait_ge(sem("toeplitz_ready"), g + 1)
                if not first:
                    dve.wait_ge(sem("y_ready"), g)
                L.do(outer(WC[:, 0, :], PWO, g, CC, 8, RE))
                outer(WC[:, 1, :], PWO, g, CC, 8, ((0, 2), (1, 0), ALU.subtract))\
                    .then_inc(sem("readout_ready"), 1)

            outputs(0, True)
            for i in L.loop(NG - 1, 6):
                dve.wait_ge(sem("readout_ready"), i + 1)
                outputs(i + 1, False)
            L.take("y_turned")
            yp = PS(0, 8, 8, NCH).rearrange("p d s n -> p d n s")
            for d in range(8):
                ins = stt(YT[:, d, :].rearrange("p (n s) -> p n s", s=8),
                          UT[:, d, 0:S].rearrange("p (n s) -> p n s", s=8), col("ssm_d", d), yp[:, d],
                          ALU.mult, ALU.add)
            L.give(ins, "y_summed")
            others(8)

            def glu(t, ps, b):
                L.do(tt(TMPX[:, b, :], ps[:, 0:S], SG[:, t, :], ALU.mult))
                g = small[:, bass.ds(t * 2 + (T0 + 96 + 2 * 16), 1)]
                return stt(X[:, t, 0:S], TMPX[:, b, :], g, X[:, t, 0:S], ALU.mult, ALU.add)

            evacuate(8, glu, 1)
            modulated(1, 1, 1)
            peer(2, 1, 0, 0)
            L.give(norm(X[:, :, 0:S], col("final", 0, 8), out_t, 8, 1.0 / D), "result_ready")


SLOTS_READ = SEGS["keys0"][0] + 4 + 2 * NEXP + 36 + 2 * NEXP + 60 + 2 * NEXP


def shape_constants():
    f = np.float32
    i = np.arange(P)
    half = 32
    inv = (10000.0 ** (-np.arange(half, dtype=f) / f(half))).astype(f)
    ang = np.arange(S, dtype=f)[None, :] * inv[:, None]
    cos, sin = np.cos(ang), np.sin(ang)
    levels = []
    for lev in range(LEVELS):
        m = 1 << lev
        levels.append(((i[:, None] // (2 * m) == i[None, :] // (2 * m)) & (i[None, :] % (2 * m) >= m)
                       & (i[:, None] % (2 * m) < m)).astype(f))
    sel = np.zeros((P, NH, P), f)
    for h in range(NH):
        sel[h, h, :] = 1.0
    cols1 = np.concatenate([
        np.tile(cos, (4, 1)), np.concatenate([-sin, sin, -sin, sin]),
        np.where(i[:, None] >= i[None, :], 0.0, -1.0e30), (i[None, :] >= i[:, None]),
        np.concatenate(levels, 1), sel.reshape(P, -1)], 1).astype(f)
    omega = (1.0 / (10000.0 ** (np.arange(256, dtype=f) / f(256)))).astype(f)
    t = np.arange(S)
    emb = []
    for pos in (t // 64, t % 64):
        a = pos.astype(f)[:, None] * omega[None, :]
        emb += [np.sin(a), np.cos(a)]
    pos = np.concatenate(emb, 1).T.reshape(KD_, P, S).transpose(1, 0, 2).astype(f)
    return np.ascontiguousarray(cols1), np.ascontiguousarray(pos)


def lay_out(a):
    f = np.float32

    def tiles(w):
        k, n = w.shape
        return w.reshape(k // P, P, n // P, P).transpose(2, 0, 1, 3).reshape(-1, P, P)

    def slots(t):
        assert t.shape[0] % 8 == 0, t.shape
        return t.reshape(-1, 8, P, P).transpose(0, 2, 1, 3).reshape(-1, P, SLOT)

    w = a["w_in"][0]
    o = np.cumsum([0, 3072, 1024, 8, 8, 384, 256, 64, 1024, 1024])
    part = [w[:, o[i]:o[i + 1]] for i in range(9)]
    ab = np.zeros((D, P), f)
    ab[:, 0:8], ab[:, 32:40] = part[2], part[3]
    kpe = part[6]
    swap = lambda m: np.concatenate([m[..., 32:], m[..., :32]], -1)
    w_in = np.concatenate([part[0], part[1], ab, part[4], part[5], kpe, kpe, swap(kpe), swap(kpe),
                           part[7], part[8]], 1)
    uq = a["w_uq"][0].reshape(384, NH, 192)
    pe = uq[:, :, 128:]
    w_uq = np.concatenate([uq[:, :, :128].reshape(384, -1), pe.reshape(384, -1), swap(pe).reshape(384, -1)], 1)
    ukv = a["w_ukv"][0].reshape(256, NH, 256)
    seg = {
        "in": slots(tiles(w_in)), "o_gdn": slots(tiles(a["w_o_gdn"][0])), "uq": slots(tiles(w_uq)),
        "kn": slots(tiles(ukv[:, :, :128].reshape(256, -1))), "v": ukv[:, :, 128:].reshape(2, P, D),
        "o_mla": slots(tiles(a["w_o_mla"][0])), "out": slots(tiles(a["w_out"][0])),
        "up": slots(tiles(a["w_up"][0])), "down": slots(tiles(a["w_down"][0])),
        "ada": np.concatenate([slots(tiles(a["ada_w_2"][l])) for l in range(2)]),
        "cm_in": slots(tiles(a["cm_w_in_2"][0])),
        "ws": a["cm_w_s_2"][0].transpose(2, 0, 1).reshape(1, P, D),
        "cm_out": slots(tiles(a["cm_w_out_2"][0])),
        "ssm_in": slots(tiles(a["ssm_w_in_2"][0])),
        "ssm_out": slots(tiles(np.concatenate([a["ssm_w_out_2"][0][:, D:], a["ssm_w_out_2"][0][:, :D]], 1))),
    }
    for l in range(2):
        seg[f"q{l}"] = slots(tiles(a["peer_w_q_2"][l]))
        keys = a["peer_keys_2"][l].reshape(16, P, 2, P).transpose(0, 2, 3, 1).reshape(32, P, P)
        seg[f"keys{l}"] = slots(keys)
    stream = np.concatenate([seg[n] for n in SEGS])
    for n, (b, c) in SEGS.items():
        assert seg[n].shape == (c, P, SLOT), (n, seg[n].shape)

    by_feature = lambda v: v.reshape(-1, P).T
    taps = lambda v: v.reshape(v.shape[0], -1, P).transpose(2, 1, 0).reshape(P, -1)
    head_col = lambda v: np.concatenate([v, np.zeros(P - NH, f)]).reshape(P, 1)
    cond = np.stack([a["c_2"][0], a["c_ctx_2"]], -1).reshape(KD_, P, 2).transpose(1, 0, 2).reshape(P, 16)
    cols = {
        "ident": np.eye(P, dtype=f), "ones": np.ones((P, P), f),
        "iota": np.tile(np.arange(P, dtype=f), (P, 1)), "norm_mix": by_feature(a["norm_mix_g"][0]),
        "conv": taps(a["conv_qkv_w"][0]), "gdn_norm": by_feature(a["gdn_norm_g"][0]),
        "a_log": head_col(a["gdn_a_log"][0]), "dt_bias": head_col(a["gdn_dt_bias"][0]),
        "q_norm": by_feature(a["mla_q_norm_g"][0]), "kv_norm": by_feature(a["mla_kv_norm_g"][0]),
        "norm_ffn": by_feature(a["norm_ffn_g"][0]), "conv_ffn": taps(a["conv_ffn_w"][0]),
        "norm_final": by_feature(a["norm_final_g"]), "ada_b": by_feature(a["ada_b_2"].reshape(-1)),
        "norm1": by_feature(a["norm1_g_2"].reshape(-1)), "norm2": by_feature(a["norm2_g_2"].reshape(-1)),
        "final": by_feature(a["final_g_2"]), "ln_g": by_feature(a["cm_ln_g_2"][0]),
        "ln_b": by_feature(a["cm_ln_b_2"][0]), "ssm_d": by_feature(a["ssm_d_2"][0]), "cond": cond,
    }
    for n, (b, c) in COLS.items():
        assert cols[n].shape == (P, c), n
    cols1, pos = shape_constants()
    feat = lambda x: x[0].T.reshape(KD_, P, S).transpose(1, 0, 2)
    states = lambda v: v.transpose(0, 2, 1).reshape(P, NG)
    mats = lambda v: v.transpose(0, 2, 1, 3).reshape(P, NG, 16)
    lam = np.stack([states(a["ssm_lam_re_2"][0]), states(a["ssm_lam_im_2"][0]),
                    np.repeat(a["ssm_log_step_2"][0][:, None, :], 64, 1).reshape(P, NG)], 1)
    ssm_b = np.stack([mats(a["ssm_b_re_2"][0]), mats(a["ssm_b_im_2"][0])], 1)
    ssm_c = np.stack([mats(a["ssm_c_re_2"][0].transpose(0, 1, 3, 2)),
                      mats(a["ssm_c_im_2"][0].transpose(0, 1, 3, 2))], 1)
    u = a["peer_u_2"].reshape(2, NEXP, P, KD_, P).transpose(0, 1, 4, 3, 2).reshape(2, NEXP, P, SLOT)
    v = a["peer_v_2"].reshape(2, NEXP, P, SLOT)
    out = {"x": feat(a["x"]), "ctx": feat(a["ctx_2"]), "cols": np.concatenate([cols[n] for n in COLS], 1),
           "cols1": cols1, "pos": pos, "bs": a["cm_b_s_2"][0].reshape(1, D), "ssm_lam": lam, "ssm_b": ssm_b,
           "ssm_c": ssm_c, "w": stream, "u": u, "v": v}
    return {n: np.ascontiguousarray(x) for n, x in out.items()}


def kernel(**inputs):
    import concourse.bacc as bacc
    from concourse.bass_utils import run_bass_kernel_spmd

    nc = bacc.Bacc("TRN2", target_bir_lowering=False, num_devices=1)
    arrays = lay_out({n: np.asarray(v) for n, v in inputs.items()})
    io = {n: nc.dram_tensor(f"in_{n}", x.shape, mybir.dt.from_np(x.dtype), kind="ExternalInput").ap()
          for n, x in arrays.items()}
    io["out"] = nc.dram_tensor("out_x", (P, KD_, S), F32, kind="ExternalOutput").ap()
    build(nc, io)
    r = run_bass_kernel_spmd(nc, [{f"in_{n}": x for n, x in arrays.items()}], core_ids=[0])
    return r.results[0]["out_x"].transpose(1, 0, 2).reshape(1, D, S).transpose(0, 2, 1)
```

```python
from contextlib import ExitStack

import numpy as np
import concourse.bass as bass
from concourse import mybir

F32 = mybir.dt.float32
U32 = mybir.dt.uint32
F32R = mybir.dt.float32r
ALU = mybir.AluOpType
ACT = mybir.ActivationFunctionType
AX = mybir.AxisListType.X

P = 128
D = 1024
KD_ = D // P
S = 256
EPS = 1e-6
NH = 8
FT = 44
FK = 22
RING = 4
SLOT = 1024
NEXP = 128
TOPK = 16
NG = 64
NCH = 32
LEVELS = 7
PI_, PM_, PO_, PB_, PC_, NPAR = 0, 16, 46, 62, 94, 142
LOWEST = -3.0e38
TWO_PI = 6.283185307179586
C1, C2 = 6.28125, 0.0019350051879882812
C3 = TWO_PI - C1 - C2
MAGIC = 12582912.0

COLS, _n = {}, 0
for _name, _w in (("ident", P), ("ones", P), ("iota", P), ("norm_mix", 8), ("conv", 96), ("gdn_norm", 1),
                  ("a_log", 1), ("dt_bias", 1), ("q_norm", 3), ("kv_norm", 2), ("norm_ffn", 8),
                  ("conv_ffn", 132), ("norm_final", 8), ("ada_b", 96), ("norm1", 16), ("norm2", 16),
                  ("final", 8), ("ln_g", 8), ("ln_b", 8), ("ssm_d", 8), ("cond", 16)):
    COLS[_name] = (_n, _w)
    _n += _w
NCOLS = _n
COLS1, _n = {}, 0
for _name, _w in (("cos", S), ("sin", S), ("neg", P), ("causal", P), ("levels", LEVELS * P), ("sel", NH * P)):
    COLS1[_name] = (_n, _w)
    _n += _w
NCOLS1 = _n

SEGS, _n = {}, 0
for _name, _w in (("in", 56), ("o_gdn", 8), ("uq", 6), ("kn", 2), ("v", 2), ("o_mla", 8), ("out", 8),
                  ("up", FT), ("down", FK), ("ada", 96), ("cm_in", 16), ("ws", 1), ("cm_out", 8),
                  ("q0", 36), ("ssm_in", 8), ("ssm_out", 16), ("q1", 36)):
    SEGS[_name] = (_n, _w)
    _n += _w
NSLOTS = _n


class Line:

    def __init__(self, eng, sem_of, chain):
        self.eng, self.sem_of, self.chain = eng, sem_of, chain
        self.base, self.k = 0, 0
        self.given, self.taken = {}, {}
        self.lin = 0
        self.slots = 0

    def do(self, ins):
        self.k += 1
        ins.then_inc(self.chain, 1)
        self.eng.wait_ge(self.chain, self.base + self.k)

    def give(self, ins, name):
        n = self.given[name] = self.given.get(name, 0) + 1
        ins.then_inc(self.sem_of(name), 1)
        self.eng.wait_ge(self.sem_of(name), n)

    def mark(self, ins, name):
        self.given[name] = self.given.get(name, 0) + 1
        ins.then_inc(self.sem_of(name), 1)

    def take(self, name):
        n = self.taken[name] = self.taken.get(name, 0) + 1
        self.eng.wait_ge(self.sem_of(name), n)

    def loop(self, count, per):
        start, b0 = self.k, self.base
        assert b0 == 0
        with self.eng.Fori(0, count) as i:
            self.base = start + i * per
            self.k = 0
            yield i
            assert self.k == per, (self.k, per)
        self.base, self.k = 0, start + count * per


def build(nc, io):
    ctx = ExitStack()
    with ctx:
        sems = {}

        def sem(name):
            if name not in sems:
                sems[name] = ctx.enter_context(nc.semaphore(name))
            return sems[name]

        sb = lambda name, shape, dt=F32: ctx.enter_context(nc.sbuf_tensor(name, shape, dt))
        T0 = NCOLS + 4864 + 64
        ring = sb("ring", [P, RING, SLOT])
        with nc.sbuf_tensor("rows_split", [P, 2, 2, SLOT], F32R) as t:
            SPL = t[:, :, :, :]
        X = sb("X", [P, KD_, 2 * S])[:, :, :]
        with nc.sbuf_tensor("input_split", [P, 2, KD_, S], F32R) as t:
            HR = t[:, :, :, :]
        H = sb("H", [P, KD_, 2 * S])[:, :, :]
        arena = sb("arena", [P, 32768])
        CFR = sb("coef_split", [P, 2, 2, S], F32R)[:, :, :, :]
        small = sb("small", [P, T0 + 576])
        psum = ctx.enter_context(nc.psum_tensor("psum", [P, 4096], F32))

        def view(t, off, *shape, parts=P):
            n = int(np.prod(shape))
            a = t[0:parts, off:off + n]
            if len(shape) == 2:
                return a.rearrange("p (a b) -> p a b", a=shape[0])
            if len(shape) == 3:
                return a.rearrange("p (a b c) -> p a b c", a=shape[0], b=shape[1])
            if len(shape) == 4:
                return a.rearrange("p (a b c d) -> p a b c d", a=shape[0], b=shape[1], c=shape[2])
            return a

        A = lambda off, *shape, parts=P: view(arena, off, *shape, parts=parts)
        PS = lambda off, *shape, parts=P: view(psum, off, *shape, parts=parts)
        bank = lambda b: psum[:, 512 * b:512 * b + 512]

        def col(name, k=0, n=1):
            o = COLS[name][0]
            return small[:, o + k:o + k + n]

        def col1(name, *shape, parts=P):
            o = NCOLS + COLS1[name][0]
            return view(small, o, *(shape or (COLS1[name][1],)), parts=parts)

        ident, ones, iota = col("ident", 0, P), col("ones", 0, P), col("iota", 0, P)
        E0 = NCOLS
        assert NCOLS + NCOLS1 <= E0 + 2816
        MOD = view(small, T0, 2, 48, 2)
        SA = view(small, T0 + 192, 2, 2, 8, 2)
        CS = view(small, T0 + 256, 8, 2)
        R1 = view(small, E0 + 2816, 512)
        R2 = view(small, E0 + 3328, 512)
        NGC = view(small, T0 + 272, 2, 8)
        TSUM = view(small, T0 + 288, 16)
        TMAX = view(small, T0 + 304, 16)
        A1C = view(small, T0 + 320, 2, NG)
        A2C = view(small, T0 + 448, 2, NG)

        QKV = A(0, 24, S)
        Q_, K_, V_ = QKV[:, 0:8, :], QKV[:, 8:16, :], QKV[:, 16:24, :]
        SQ = A(6144, 16, S)
        TT = A(6144, 16, P)
        TI = A(8192, 16, P)
        OG = A(8192, 8, S)
        GT = A(10240, 8, S)
        GB = A(12288, 16, S)
        MISC = A(16384, 8, S)
        AB, CQ, CKV, KP, KPS = MISC[:, 0, :], MISC[:, 1:4, :], MISC[:, 4:6, :], MISC[:, 6, :], MISC[:, 7, :]
        BETA = A(18432, 8, S)
        ML = A(18432, 16, P)
        DEC = A(20480, 8, S)
        AM = A(20480, 16, P)
        EGB = A(22528, 8, P)
        EDB = A(23552, 8, P)
        VT = A(22528, 16, P)
        KDC = A(24576, 8, P)
        QD = A(25600, 8, P)
        KBG = A(26624, 8, P)
        LT = A(27648, 16, P)
        AT = A(29696, 16, P)
        ROWS = A(31744, 4, S, parts=8)
        VN0, VN1 = A(18432, 8, P), A(19456, 8, P)
        S1, RR = A(20480, 8, P), A(21504, 8, P)
        SQO = A(27648, 8, S)
        RSO = A(24576, 8, S)
        YA = A(0, 8, S)
        SQM = A(2048, 3, S)
        QN = A(4096, 8, S)
        QP = A(6144, 4, S)
        QPS = A(7168, 4, S)
        QPR = A(6144, 8, S)
        KN = A(8192, 8, S)
        MG = A(10240, 8, S)
        VM = A(18432, 2, D)
        SC = A(20480, 8, 384)
        PT = A(23552, 8, 384)
        OB = A(26624, 8, S)
        TMP = A(28672, 4, S)
        KPP = A(29696, 2, S)
        TME = A(28672, 2, S)
        UF = A(0, FT, S)
        SQX = A(12288, 8, S)
        SQX2 = A(0, 8, 2 * S)
        Z = A(0, 16, 512)
        SQZ = A(8192, 8, 512)
        ZT = A(12288, 32, P)
        BS = A(31744, D, parts=1)
        MR = A(0, 12, D, parts=2)
        QT = A(0, 32, S)
        HT = A(28672, 8, S)
        SCO = A(8192, 2, 16, P)
        SV = A(12288, 2, 16, 16)
        IDX = A(12800, 2, 16, 16).bitcast(U32)
        IDF = A(13312, 2, 16, 16)
        WK = A(24576 + 768, 8, P)
        WK2 = A(24576 + 1792, 4, 256)
        CAND = A(14336, 16, 256)
        TS = A(18432, 16, 16)
        TC = A(18688, 16, 16).bitcast(U32)
        CI = A(18944, 2, 256).bitcast(U32)
        CF_ = A(19456, 2, 256)
        OH = A(20480, 256, 16)
        KK = A(24576, 3, 256)
        G = A(0, NEXP, S)
        K3 = view(small, E0, 3, S)
        EA = view(small, E0 + 768, 2, 8, P)
        EB = view(small, E0 + 2816, 2, 8, P)
        AC = view(small, E0 + 768, 2, S)
        CF = view(small, E0 + 1280, 2, S)
        KS = view(small, E0 + 4864, 2, 3, 8)
        PAR = A(20480, NG, NPAR)
        RAW = A(29568, 2, NG, 16)
        RAWC = A(12288, 2, NG, 16)
        PW = A(14336, 9, 2, NG)
        TP = A(16384, 24, NG)
        LAM = A(16384 + 24 * NG, 3, NG)
        TB1, TB2 = A(18432, NG, 16), A(19456, NG, 16)
        G0 = E0 + 1792
        PARS = view(small, G0, NPAR)
        WCI = view(small, G0 + 142, 2, P)
        WCM = view(small, G0 + 398, 2, P)
        WW = view(small, G0 + 654, 2, 240)
        WT1 = view(small, G0 + 1134, 240)
        WT2 = view(small, G0 + 1374, 240)
        STGI = view(small, G0 + 1614, 2, P)
        STGK = view(small, G0 + 1870, 2, 16)
        UT = A(0, 8, 512)
        UN = A(4096, NG, 8, 16, parts=64)
        XS = A(4096, 64, 2, NG)
        YN = A(4096, 8, D, parts=NCH)
        UG = A(12288, NG, 64)
        HS = A(16384, NCH, 2, NG)
        MB = A(20480, 2, 8, 2, P)
        TOEP = A(24576, NG, 8, 16)
        HST = view(small, E0, 2, NG)
        ST1 = view(small, E0 + 128, 2, NG)
        ST2 = view(small, E0 + 256, 2, NG)
        YT = A(20480, 8, S)
        SG = A(22528, 8, S)
        TMPX = A(24576, 2, S)
        CT = CF
        out_t = A(0, 8, S)

        nseg = lambda name: SEGS[name]

        stream = []

        def seg(*names):
            a = nseg(names[0])[0]
            b = nseg(names[-1])[0] + nseg(names[-1])[1]
            stream.append(("w", a, b - a))

        seg("in", "q0")
        stream.append(("uv", 0, True))
        seg("q0", "q0")
        stream.append(("uv", 0, False))
        seg("ssm_in", "q1")
        stream.append(("uv", 1, True))

        block = ctx.enter_context(nc.Block())

        @block.gpsimd
        def _(pool):
            def park(n):
                pool.wait_ge(sem("input_parts"), n + 1)
                pool.dma_start(io["parked"], X.rearrange("p d t -> p (d t)")).then_inc(sem("x_parked"), 16)
                pool.wait_ge(sem("x_parked"), 16 * n + 16)
                pool.wait_ge(sem("coef_used"), (NEXP, 3 * NEXP)[n])
                pool.dma_start(X.rearrange("p d t -> p (d t)"), io["parked"]).then_inc(sem("x_back"), 16)

            pool.dma_start(H[:, :, S:2 * S], io["pos"]).then_inc(sem("pos_loaded"), 16)
            pool.wait_ge(sem("x_normed"), 1)
            pool.dma_start(RAW, io["ssm_b"]).then_inc(sem("ssm_loaded"), 16)
            pool.dma_start(RAWC, io["ssm_c"]).then_inc(sem("ssm_loaded"), 16)
            pool.dma_start(LAM, io["ssm_lam"]).then_inc(sem("ssm_loaded"), 16)
            pool.dma_start(BS, io["bs"]).then_inc(sem("bs_loaded"), 16)
            pool.wait_ge(sem("par_ready"), 1)
            pool.dma_start(io["par"], PAR.rearrange("p g n -> p (g n)")).then_inc(sem("par_stored"), 16)
            park(0)
            pool.wait_ge(sem("acc_evacuated"), 2)
            pool.wait_ge(sem("inj_stored"), 16 * NG)
            pool.wait_ge(sem("cm_stored"), 16 * NG)
            pool.wait_ge(sem("lags_stored"), 32 * NG)

            def batch(src, q):
                pool.dma_start(MB[:, q % 2].rearrange("p g r n -> p g (r n)"), src[8 * (q % 8):8 * (q % 8) + 8].rearrange("g p n -> p g n"))\
                    .then_inc(sem(f"batch_loaded{q % 2}"), 16)

            batch(io["inj"], 0)
            batch(io["inj"], 1)
            for t in range(8):
                for q in range(4):
                    pool.dma_start(TOEP[:, 16 * q:16 * q + 16, t, :],
                                   io["lags"][16 * q:16 * q + 16, 16 * (7 - t):16 * (7 - t) + P, :]
                                   .rearrange("g p c -> p g c")).then_inc(sem("toep_loaded"), 16)
            for q in range(2, 16):
                pool.wait_ge(sem("injected" if q < 10 else "y_ready"), q - 1 if q < 10 else q - 9)
                batch(io["inj"] if q < 8 else io["cm"], q)
            park(1)

        @block.sync
        def _(sp):
            def load(dst, src, name="inputs_loaded"):
                sp.dma_start(dst, src).then_inc(sem(name), 16)

            load(X[:, :, 0:S], io["x"])
            load(small[:, 0:NCOLS], io["cols"])
            load(small[:, NCOLS:NCOLS + NCOLS1], io["cols1"])
            load(X[:, :, S:2 * S], io["ctx"])
            n = 0
            nb = 0
            fast = 0
            behind = 0

            def fill(src, m):
                sp.dma_start(ring[:, m % RING, :], src).then_inc(sem(f"slot_loaded{m % RING}"), 16)

            def one(src):
                nonlocal n, nb, behind
                if behind:
                    sp.wait_ge(sem("u_low"), NEXP * fast)
                    sp.wait_ge(sem("v_low"), NEXP * fast)
                    behind -= 1
                elif n >= RING:
                    sp.wait_ge(sem("slot_begun"), nb - RING + 2)
                fill(src, n)
                n, nb = n + 1, nb + 1

            for kind, a, split in stream:
                if kind == "w":
                    count = split
                    while count % RING or n < RING or behind:
                        one(io["w"][a])
                        a, count = a + 1, count - 1
                    with sp.Fori(0, count // RING) as i:
                        for b in range(RING):
                            sp.wait_ge(sem("slot_begun"), i * RING + (nb + b - RING + 2))
                            fill(io["w"][i * RING + (a + b)], n + b)
                    n, nb = n + count, nb + count
                    continue
                u, v = io["u"][a], io["v"][a]
                one(u[0])
                one(u[1])
                one(v[0])
                if not split:
                    with sp.Fori(0, (NEXP - 2) // 2) as i:
                        for b in range(2):
                            sp.wait_ge(sem("slot_begun"), i * 4 + (nb + 2 * b - RING + 2))
                            fill(u[i * 2 + (b + 2)], n + 2 * b)
                            sp.wait_ge(sem("slot_begun"), i * 4 + (nb + 2 * b - RING + 3))
                            fill(v[i * 2 + (b + 1)], n + 2 * b + 1)
                    n, nb = n + 2 * (NEXP - 2), nb + 2 * (NEXP - 2)
                    one(v[NEXP - 1])
                    continue
                nb -= 3
                n0 = NEXP * fast
                for j in (1, 2):
                    sp.wait_ge(sem("u_low"), n0 + j)
                    fill(u[j + 1], n)
                    if j == 2:
                        sp.wait_ge(sem("v_low"), n0 + 1)
                    fill(v[j], n + 1)
                    n += 2
                with sp.Fori(1, (NEXP - 2) // 2) as i:
                    for b in range(2):
                        sp.wait_ge(sem("u_low"), i * 2 + (n0 + b + 1))
                        fill(u[i * 2 + (b + 2)], n + 2 * b)
                        sp.wait_ge(sem("v_low"), i * 2 + (n0 + b))
                        fill(v[i * 2 + (b + 1)], n + 2 * b + 1)
                n += 2 * (NEXP - 4)
                fast += 1
                sp.wait_ge(sem("v_low"), NEXP * fast - 2)
                fill(v[NEXP - 1], n)
                n += 1
                behind = RING
            sp.wait_ge(sem("result_ready"), 1)
            load(io["out"], out_t, "result_stored")
            sp.wait_ge(sem("result_stored"), 16)

        @block.tensor
        def _(pe):
            L = Line(pe, sem, sem("pe_chain"))
            mm = pe.matmul

            def arrived(w):
                pe.wait_ge(sem(f"slot_loaded{w % RING}"), 16 * (w // RING + 1))

            def evacuated():
                pe.wait_ge(sem("lin_free"), L.lin)

            def linear(tiles, kt, rhs, n, m=P):
                w0, l0 = L.slots, L.lin
                if l0:
                    evacuated()
                begun = [False]

                def tile(t, static=True):
                    for k in range(kt):
                        s = t * kt + k
                        if s % 8 == 0:
                            begun[0] = True
                            if static:
                                arrived(w0 + s // 8)
                        last = mm(bank(t % 2)[0:m, 0:n], ring[:, (w0 + s // 8) % RING, (s % 8) * P:(s % 8) * P + m],
                                  rhs[:, k, 0:n], start=(k == 0), stop=(k == kt - 1))
                        if begun[0] and k < kt - 1:
                            last.then_inc(sem("slot_begun"), 1)
                            begun[0] = False
                    last.then_inc(sem("lin_ready"), 1)

                looped = kt == 8 and tiles % RING == 0 and tiles >= 8
                for t in range(RING if looped else tiles):
                    if t >= 2:
                        pe.wait_ge(sem("lin_free"), l0 + t - 1)
                    tile(t)
                if looped:
                    with pe.Fori(1, tiles // RING) as i:
                        for b in range(RING):
                            w = w0 + b
                            pe.wait_ge(sem("lin_free"), i * RING + (l0 + b - 1))
                            pe.wait_ge(sem(f"slot_loaded{w % RING}"), i * 16 + 16 * (w // RING + 1))
                            tile(b, False)
                assert not begun[0]
                L.lin += tiles
                L.slots += tiles * kt // 8

            def rowsum(src, kt, n, ready="squares"):
                if ready:
                    L.take(ready)
                for k in range(kt):
                    last = mm(bank(7)[:, 0:n], ones, src[:, k, 0:n], start=(k == 0), stop=(k == kt - 1))
                L.mark(last, "rowsum")

            pe.wait_ge(sem("inputs_loaded"), 64)
            rowsum(SQX, 8, S)
            L.take("normed")
            linear(24, 8, H, S)
            linear(8, 8, H, S)
            linear(8, 8, H, S)
            linear(16, 8, H, S)
            evacuated()
            L.take("head_squares")
            for b in range(8):
                last = mm(bank(b), ones, SQ[:, 2 * b:2 * b + 2, :], start=True, stop=True)
            L.mark(last, "head_sums")
            L.take("row_exps")
            L.take("head_sums_used")
            sel = col1("sel", NH, P, parts=8)
            for r in range(2):
                for h in range(NH):
                    last = mm(PS(2048 * r + S * h, S), sel[:, h, :], ROWS[:, r, :], start=(h % 2 == 0), stop=True,
                              skip_group_check=True)
            L.mark(last, "rows_spread")
            L.take("beta_evacuated")
            L.take("decay_evacuated")
            for h in range(NH):
                mm(PS(P * h, P), sel[:, h, :], ROWS[:, 2, P:S], start=(h % 4 == 0), stop=True, skip_group_check=True)
                mm(PS(1024 + P * h, P), sel[:, h, :], ROWS[:, 3, 0:P], start=(h % 4 == 0), stop=True,
                   skip_group_check=True)
            for c in range(2):
                last = pe.transpose(PS(2048 + 8 * c, 8), ROWS[:, 1, P * c:P * c + P], ident[0:8, 0:8])
            L.mark(last, "exps_spread")
            L.take("gdn_operands")
            for h in range(NH):
                for c in range(2):
                    j, t = 2 * h + c, slice(P * c, P * c + P)
                    mm(PS(P * j, P), K_[:, h, t], K_[:, h, t], start=(j % 4 == 0), stop=True, skip_group_check=True)
                    last = mm(PS(2048 + P * j, P), K_[:, h, t], Q_[:, h, t], start=(j % 4 == 0), stop=True,
                              skip_group_check=True)
            L.mark(last, "kk_ready")
            L.take("kk_evacuated")
            for h in range(NH):
                for c in range(2):
                    pe.transpose(PS(P * (2 * h + c), P), V_[:, h, P * c:P * c + P], ident)
                last = pe.transpose(PS(2048 + P * h, P), KDC[:, h, :], ident)
            L.mark(last, "vt_ready")
            L.take("vt_evacuated")
            L.take("inverse_begun")
            for j in range(16):
                last = pe.transpose(PS(P * j, P), TT[:, j, :], ident)
            L.mark(last, "inverse_turned")
            for lev in range(1, LEVELS):
                L.take("level_masked")
                for j in range(16):
                    last = mm(PS(P * j, P), ML[:, j, :], TI[:, j, :], start=(j % 4 == 0), stop=True,
                              skip_group_check=True)
                L.mark(last, "level_inner")
                L.take("level_inner_evacuated")
                for j in range(16):
                    if lev < LEVELS - 1:
                        mm(PS(2048 + P * j, P), TT[:, j, :], AM[:, j, :], start=(j % 4 == 0), stop=True,
                           skip_group_check=True)
                    last = mm(PS(P * j, P), AM[:, j, :], TT[:, j, :], start=(j % 4 == 0), stop=True,
                              skip_group_check=True)
                L.mark(last, "level_outer")
            L.take("inverse_ready")
            vt = VT.rearrange("p (h c) d -> p h c d", c=2)
            tt = TT.rearrange("p (h c) d -> p h c d", c=2)
            at = AT.rearrange("p (h c) d -> p h c d", c=2)

            def heads(off, *pairs):
                for h in range(NH):
                    for n, (a, b) in enumerate(pairs):
                        last = mm(PS(off + P * h, P), a[:, h, :], b[:, h, :], start=(h % 4 == 0 and n == 0),
                                  stop=(n == len(pairs) - 1), skip_group_check=True)
                return last

            L.mark(heads(0, (tt[:, :, 0, :], vt[:, :, 0, :])), "new0_ready")
            L.take("new0_evacuated")
            heads(1024, (KDC, VN0))
            L.mark(heads(2048, (VN0, at[:, :, 0, :])), "state_ready")
            L.take("state_evacuated")
            L.mark(heads(0, (KBG, S1)), "old_value_ready")
            L.take("residual_ready")
            L.mark(heads(1024, (tt[:, :, 1, :], RR)), "new1_ready")
            L.take("new1_evacuated")
            for h in range(NH):
                mm(PS(3072 + P * h, P), S1[:, h, :], QD[:, h, :], start=(h % 4 == 0), stop=False,
                   skip_group_check=True)
                last = mm(PS(3072 + P * h, P), VN1[:, h, :], at[:, h, 1, :], start=False, stop=True,
                          skip_group_check=True)
            L.mark(last, "gdn_out1")
            L.take("squares")
            for b in range(4):
                last = mm(bank(b), ones, SQO[:, 2 * b:2 * b + 2, :], start=True, stop=True)
            L.mark(last, "rowsum")
            L.take("gdn_gated")
            linear(8, 8, OG, S)
            rowsum(SQM, 3, S)
            rowsum(SQM, 2, S)
            L.take("latent_normed")
            linear(8, 3, CQ, S)
            linear(8, 3, CQ, S)
            linear(8, 2, CKV, S)
            for k in range(2):
                arrived(L.slots)
                for i in range(2):
                    for f in range(2):
                        last = mm(bank(2 + 2 * i + f), CKV[:, k, P * i:P * i + P],
                                  ring[:, L.slots % RING, 512 * f:512 * f + 512], start=(k == 0), stop=(k == 1))
                        if i == 0 and f == 0:
                            last.then_inc(sem("slot_begun"), 1)
                L.slots += 1
            L.mark(last, "v_ready")
            L.take("rope_ready")
            L.take("v_evacuated")
            evacuated()
            for h in range(NH):
                for c, (a, n) in enumerate(((0, P), (P, S))):
                    q = slice(P * c, P * c + P)
                    mm(bank(h)[:, a:a + n], QN[:, h, q], KN[:, h, 0:n], start=(c == 0), stop=False,
                       skip_group_check=True)
                    last = mm(bank(h)[:, a:a + n], QP[:, h // 2, q], KPP[:, h % 2, 0:n], start=False, stop=True,
                              skip_group_check=True)
            L.mark(last, "scores_ready")
            L.take("probs_ready")
            for h in range(NH):
                for j in range(3):
                    last = pe.transpose(bank(h)[:, P * j:P * j + P], SC[:, h, P * j:P * j + P], ident)
            L.mark(last, "probs_turned")
            L.take("probs_evacuated")
            for h in range(NH):
                v = slice(P * h, P * h + P)
                o = PS(S * h, S)
                mm(o[:, 0:P], VM[:, 0, v], PT[:, h, 0:P], start=(h % 2 == 0), stop=True, skip_group_check=True)
                mm(o[:, P:S], VM[:, 0, v], PT[:, h, P:S], start=False, stop=False, skip_group_check=True)
                last = mm(o[:, P:S], VM[:, 1, v], PT[:, h, S:S + P], start=False, stop=True, skip_group_check=True)
            L.mark(last, "attention_out")
            L.take("attention_ready")
            linear(8, 8, OB, S)
            linear(8, 8, MG, S)
            rowsum(SQX, 8, S)
            L.take("normed")
            linear(FT, 8, H, S)
            L.take("ffn_inner")
            linear(8, FK, UF, S)
            rowsum(SQX, 8, S)
            L.take("cond_silu")
            w0 = L.slots

            def ada(q, i=None):
                for k in range(8):
                    w = w0 + 8 * q + k
                    if i is None:
                        arrived(w)
                    else:
                        pe.wait_ge(sem(f"slot_loaded{w % RING}"), i * 64 + 16 * (w // RING + 1))
                    for f in range(2):
                        last = mm(bank(2 * (q % 2) + f)[0:2, :], CS[:, k, :],
                                  ring[:, w % RING, 512 * f:512 * f + 512], start=(k == 0), stop=(k == 7))
                        if f == 0:
                            last.then_inc(sem("slot_begun"), 1)
                last.then_inc(sem("ada_ready"), 1)

            ada(0)
            ada(1)
            with pe.Fori(1, 6) as i:
                for b in range(2):
                    pe.wait_ge(sem("ada_evacuated"), i * 2 + (b - 1))
                    ada(b, i)
            L.slots += 96
            pe.wait_ge(sem("ada_evacuated"), 12)
            for t in range(96):
                last = pe.transpose(PS(2048 + 2 * t, 2), MR[:, t // 8, P * (t % 8):P * (t % 8) + P], ident[0:2, 0:2])
            L.mark(last, "mods_ready")

            def split_experts(n0, s0):
                parts = ((0, 0), (0, 1), (1, 0))
                L.take("input_parts")

                def up(j, b, first=False):
                    if not first:
                        pe.wait_ge(sem("gelu_done"), j + (n0 - 1))
                    pe.wait_ge(sem("u_low"), j + (s0 + 1))
                    for k in range(8):
                        for w, x in parts:
                            last = mm(bank(b)[:, 0:S], SPL[:, 0, w, P * k:P * k + P], HR[:, x, k, :],
                                      start=(k == 0 and (w, x) == (0, 0)), stop=(k == 7 and w == 1))
                    last.then_inc(sem("up_ready"), 1)

                def down(j, b, first=False):
                    pe.wait_ge(sem("coef_ready"), j + (n0 + 1))
                    pe.wait_ge(sem("v_low"), j + (s0 + 1))
                    for d in range(8):
                        for w, x in parts:
                            last = mm(PS(1024 + S * d, S), SPL[:, 1, w, P * d:P * d + P], CFR[:, b, x, :],
                                      start=(first and d % 2 == 0 and (w, x) == (0, 0)), stop=False,
                                      skip_group_check=True)
                    last.then_inc(sem("coef_used"), 1)

                up(0, 0, True)
                up(1, 1, True)
                down(0, 0, True)
                with pe.Fori(0, (NEXP - 2) // 2) as i:
                    for b in range(2):
                        up(i * 2 + (b + 2), b)
                        down(i * 2 + (b + 1), 1 - b)
                down(NEXP - 1, 1)

            def peer(p, off):
                rowsum(SQX2, 8, S)
                L.take("normed")
                for s in range(4):
                    linear(8, 8, HT if p != 1 else H, S)
                    evacuated()
                    if s >= 2:
                        L.take("key_scores_used")
                    arrived(L.slots)
                    for q in range(4):
                        for i in range(2):
                            for d in range(2):
                                last = mm(bank(2 + 2 * (s % 2) + i)[:, P * q:P * q + P],
                                          QT[:, 2 * (4 * s + q) + d, P * i:P * i + P],
                                          ring[:, L.slots % RING, P * (2 * q + d):P * (2 * q + d) + P],
                                          start=(q == 0 and d == 0), stop=(d == 1), skip_group_check=True)
                                if q == 0 and i == 0 and d == 0:
                                    last.then_inc(sem("slot_begun"), 1)
                    L.slots += 1
                    L.mark(last, "key_scores")
                L.take("key_scores_used")
                L.take("key_scores_used")
                L.take("chosen")
                for m in range(3):
                    for i in range(2):
                        last = pe.transpose(PS(S * m + P * i, P), KK[:, m, P * i:P * i + P], ident)
                L.mark(last, "chosen_turned")
                L.take("chosen_evacuated")

                def build(n, b, first):
                    pe.wait_ge(sem("onehots_ready"), n + 1)
                    if not first:
                        pe.wait_ge(sem("gates_evacuated"), n - 1)
                    for t in range(8):
                        last = mm(PS(1024 * b + P * t, P), EB[:, b, t, :], EA[:, b, t, :], start=(t % 4 == 0),
                                  stop=True, skip_group_check=True)
                    last.then_inc(sem("gates_built"), 1)

                for b in range(2):
                    build(32 * p + b, b, True)
                with pe.Fori(1, 16) as i:
                    for b in range(2):
                        build(i * 2 + (32 * p + b), b, False)
                pe.wait_ge(sem("gates_evacuated"), 32 * p + 32)

                w0, n0 = L.slots, NEXP * p
                if p != 1:
                    split_experts(n0, NEXP * (p // 2))
                    L.slots += 2 * NEXP
                    L.take("acc_evacuated")
                    return

                def up(j, b, r, wait, first=False):
                    wait()
                    if not first:
                        pe.wait_ge(sem("gelu_done"), j + (n0 - 1))
                    for k in range(8):
                        last = mm(bank(b)[:, 0:S], ring[:, r % RING, P * k:P * k + P], H[:, k, 0:S],
                                  start=(k == 0), stop=(k == 7))
                        if k == 0:
                            last.then_inc(sem("slot_begun"), 1)
                    last.then_inc(sem("up_ready"), 1)

                def down(j, b, r, wait, first=False):
                    wait()
                    pe.wait_ge(sem("coef_ready"), j + (n0 + 1))
                    for d in range(8):
                        last = mm(PS(1024 + S * d, S), ring[:, r % RING, P * d:P * d + P], CF[:, b, :],
                                  start=(first and d % 2 == 0), stop=False, skip_group_check=True)
                        if d == 0:
                            last.then_inc(sem("slot_begun"), 1)
                    last.then_inc(sem("coef_used"), 1)

                def injection(g, first=False):
                    pe.wait_ge(sem("inj_ready"), g + 1)
                    if not first:
                        pe.wait_ge(sem("inj_evacuated"), g)
                    for r in range(2):
                        last = pe.transpose(bank(6)[:, P * r:P * r + P], WCI[:, r, :], ident)
                    last.then_inc(sem("inj_turned"), 1)

                def lags(g, first=False):
                    pe.wait_ge(sem("lags_ready"), g + 1)
                    if not first:
                        pe.wait_ge(sem("lags_evacuated"), g)
                    for m in range(2):
                        for r in range(2):
                            last = mm(bank(7)[:, 16 * m:16 * m + 16], WW[:, r, 112 * m:112 * m + P],
                                      PARS[:, PC_ + 32 * r:PC_ + 32 * r + 16], start=(m == 0 and r == 0),
                                      stop=(r == 1), skip_group_check=True)
                    last.then_inc(sem("lags_turned"), 1)

                up(0, 0, w0, lambda: arrived(w0), True)
                up(1, 1, w0 + 1, lambda: arrived(w0 + 1), True)
                down(0, 0, w0 + 2, lambda: arrived(w0 + 2), True)
                if p == 1:
                    injection(0, True)
                    lags(0, True)
                w1 = w0 + 3
                with pe.Fori(0, (NEXP - 2) // 2) as i:
                    def arrived_in_loop(w):
                        pe.wait_ge(sem(f"slot_loaded{w % RING}"), i * 16 + 16 * (w // RING + 1))

                    for b in range(2):
                        w = w1 + 2 * b
                        up(i * 2 + (b + 2), b, w, lambda: arrived_in_loop(w))
                        down(i * 2 + (b + 1), 1 - b, w + 1, lambda: arrived_in_loop(w + 1))
                        if p == 1:
                            (lags if b else injection)(i + 1)
                w = w1 + 2 * (NEXP - 2)
                down(NEXP - 1, 1, w, lambda: arrived(w))
                L.slots = w + 1
                L.take("acc_evacuated")

            rowsum(SQX2, 8, 512)
            L.take("normed")
            linear(16, 8, H, 512)
            evacuated()
            rowsum(Z[:, 8:16, :], 8, 512, None)
            rowsum(SQZ, 8, 512)
            L.take("v_normed")
            for h in range(8):
                for n in range(4):
                    last = pe.transpose(PS(P * (4 * h + n), P), Z[:, 8 + h, P * n:P * n + P], ident)
            L.mark(last, "v_turned")
            L.take("v_turned_evacuated")
            arrived(L.slots)
            pe.wait_ge(sem("bs_loaded"), 16)
            for h in range(8):
                for n in range(4):
                    o = PS(P * (4 * h + n), P)
                    last = mm(o, ZT[:, 4 * h + n, :], ring[:, L.slots % RING, P * h:P * h + P], start=(n == 0),
                              stop=False, skip_group_check=True)
                    if h == 0 and n == 0:
                        last.then_inc(sem("slot_begun"), 1)
                    last = mm(o, ones[0:1, :], BS[:, P * h:P * h + P], start=False, stop=True,
                              skip_group_check=True)
            L.slots += 1
            L.mark(last, "mixed")
            L.take("mixed_used")
            linear(8, 8, Z, 512)
            peer(0, 0)
            peer(1, S)
            rowsum(SQX2, 8, 512)
            L.take("normed")
            linear(8, 8, H, 512)
            evacuated()
            for q in range(2):
                if q:
                    L.take("tokens_evacuated")
                for d in range(4):
                    for s in range(8):
                        last = pe.transpose(PS(P * (8 * d + s), P, parts=64),
                                            UT[:, 4 * q + d, s:512:8], ident)
                L.mark(last, "tokens_turned")
            L.take("tokens_evacuated")
            for g in range(NG):
                last = pe.transpose(PS(64 * g, 64), UN[:, g, :, :].rearrange("p s c -> p (s c)"), ident[0:64, 0:64])
            L.mark(last, "groups_turned")
            L.take("groups_ready")

            def batch_arrived(q):
                pe.wait_ge(sem(f"batch_loaded{q % 2}"), 16 * (q // 2 + 1))

            for q in range(8):
                batch_arrived(q)
                if q >= 4:
                    L.take("injected_evacuated")
                for g in range(8):
                    for r in range(2):
                        last = mm(PS(1024 * (q % 4) + P * g + 64 * r, 64), MB[:, q % 2, g, r, :],
                                  UG[:, 8 * q + g, :], start=(g % 4 == 0 and r == 0), stop=True,
                                  skip_group_check=True)
                L.mark(last, "injected")
            for q in range(4):
                L.take("injected_evacuated")
            L.take("scanned")
            pe.wait_ge(sem("toep_loaded"), 16 * 32)
            for q in range(8):
                batch_arrived(8 + q)
                if q >= 4:
                    L.take("y_evacuated")
                for g in range(8):
                    gg = 8 * q + g
                    o = PS(1024 * (q % 4) + P * g, P, parts=NCH)
                    mm(o, UG[:, gg, 0:NCH], TOEP[:, gg].rearrange("p t c -> p (t c)"), start=(g % 4 == 0),
                       stop=False, skip_group_check=True)
                    for r in range(2):
                        last = mm(o, HS[:, :, r, gg], MB[:, q % 2, g, r, :], start=False, stop=(r == 1),
                                  skip_group_check=True)
                L.mark(last, "y_ready")
            for q in range(4):
                L.take("y_evacuated")
            for d in range(8):
                for s in range(8):
                    last = pe.transpose(PS(NCH * (8 * d + s), NCH), YN[:, s, P * d:P * d + P],
                                        ident[0:NCH, 0:NCH])
            L.mark(last, "y_turned")
            L.take("y_gelu")
            linear(8, 8, YT, S)
            linear(8, 8, YT, S)
            peer(2, 0)
            rowsum(SQX, 8, S)
            assert L.slots == SLOTS_READ

        @block.scalar
        def _(act):
            L = Line(act, sem, sem("act_chain"))
            f = act.activation
            copy = lambda o, i: f(o, i, ACT.Copy)

            def evacuate(tiles, fn):
                l0 = L.lin
                turns = L.loop(tiles // 2, 0) if tiles >= 8 else [0]
                for i in turns:
                    for b in range(2):
                        act.wait_ge(sem("lin_ready"), i * 2 + (l0 + b + 1))
                        fn(i * 2 + b, bank(b)).then_inc(sem("lin_free"), 1)
                act.wait_ge(sem("lin_free"), l0 + tiles)
                L.lin += tiles

            def others(tiles):
                L.lin += tiles

            def norm(src, dst, ready):
                if ready:
                    L.take(ready)
                L.give(f(dst, src, ACT.Square), "squares")
                root(R1[:, 0:src.shape[2]], R2[:, 0:src.shape[2]])

            def root(a, b):
                L.take("var")
                L.give(f(b, a, ACT.Sqrt), "rstd")

            act.wait_ge(sem("inputs_loaded"), 64)
            L.give(f(CS, col("cond", 0, 16).rearrange("p (a b) -> p a b", b=2), ACT.Silu), "cond_silu")
            norm(X[:, :, 0:S], SQX, None)
            others(24)
            evacuate(8, lambda t, ps: f(GT[:, t, :], ps[:, 0:S], ACT.Silu))
            others(8)
            evacuate(16, lambda t, ps: f(GB[:, t, :], ps[:, 0:S], ACT.Sigmoid))
            act.wait_ge(sem("lin_free"), L.lin)
            a = AB[0:8, :]
            L.do(f(ROWS[:, 0, :], AB[32:40, :], ACT.Sigmoid))
            L.do(f(QKV, QKV, ACT.Silu))
            L.give(f(SQ, QKV[:, 0:16, :], ACT.Square), "head_squares")
            L.do(f(a, a, ACT.Identity, bias=col("dt_bias")[0:8, :]))
            L.do(f(ROWS[:, 3, :], a, ACT.Abs))
            L.do(f(ROWS[:, 3, :], ROWS[:, 3, :], ACT.Exp, scale=-1.0))
            L.do(f(ROWS[:, 3, :], ROWS[:, 3, :], ACT.Ln, bias=1.0))
            L.give(f(TSUM[0:8, 0:1], col("a_log")[0:8, :], ACT.Exp), "softplus_parts")
            L.take("decay_rows")
            L.do(f(ROWS[:, 2, :], ROWS[:, 1, :], ACT.Exp))
            L.give(f(ROWS[:, 3, :], ROWS[:, 3, :], ACT.Exp), "row_exps")
            L.take("head_var")
            L.give(f(SQ, SQ, ACT.Sqrt), "head_rstd")
            L.take("rows_spread")
            L.give(copy(BETA, PS(0, 8, S)), "beta_evacuated")
            L.take("exps_spread")
            L.do(copy(EGB, PS(0, 8, P)))
            L.give(copy(EDB, PS(1024, 8, P)), "exps_evacuated")
            L.take("decay_args")
            L.give(f(DEC, DEC, ACT.Exp), "decay_exp")
            L.take("vt_ready")
            L.do(copy(VT, PS(0, 16, P)))
            L.give(copy(KDC, PS(2048, 8, P)), "vt_evacuated")
            L.take("gdn_out")
            L.give(f(SQO, OG, ACT.Square), "squares")
            root(RSO, RSO)
            others(8)
            act.wait_ge(sem("lin_free"), L.lin)
            L.give(f(SQM, CQ, ACT.Square), "squares")
            root(R1[:, 0:S], R2[:, 0:S])
            L.take("latent_q_normed")
            L.give(f(SQM[:, 0:2, :], CKV, ACT.Square), "squares")
            root(R1[:, 0:S], R2[:, 0:S])
            evacuate(8, lambda t, ps: copy(QN[:, t, :], ps[:, 0:S]))
            others(8)
            evacuate(8, lambda t, ps: copy(KN[:, t, :], ps[:, 0:S]))
            L.take("v_ready")
            L.give(copy(VM, PS(1024, 2, D)), "v_evacuated")
            L.take("scores_shifted")
            L.give(f(SC, SC, ACT.Exp), "probs_exp")
            L.take("probs_turned")
            L.give(copy(PT, PS(0, 8, 512)[:, :, 0:384]), "probs_evacuated")
            others(16)
            act.wait_ge(sem("lin_free"), L.lin)
            norm(X[:, :, 0:S], SQX, None)
            others(FT)
            act.wait_ge(sem("lin_free"), L.lin)
            L.give(f(UF[:, 0:FK, :], UF[:, 0:FK, :], ACT.Silu), "ffn_gate")
            others(8)
            act.wait_ge(sem("lin_free"), L.lin)
            norm(X[:, :, 0:S], SQX, None)

            def split_experts(n0, s0, w0):
                def high_u(j, w, i=None, first=False):
                    arrived(w, i)
                    if not first:
                        act.wait_ge(sem("up_ready"), j + n0)
                    copy(SPL[:, 0, 0, :], ring[:, w % RING, :]).then_inc(sem("u_high"), 1)

                def high_v(j, w, i=None, first=False):
                    arrived(w, i)
                    if not first:
                        act.wait_ge(sem("coef_used"), j + n0)
                    copy(SPL[:, 1, 0, :], ring[:, w % RING, :]).then_inc(sem("v_high"), 1)

                def arrived(w, i):
                    v = 16 * (w // RING + 1)
                    act.wait_ge(sem(f"slot_loaded{w % RING}"), v if i is None else i * 16 + v)

                def gelu(j, b, first=False):
                    act.wait_ge(sem("up_ready"), j + (n0 + 1))
                    if not first:
                        act.wait_ge(sem("coef_ready"), j + (n0 - 1))
                    f(AC[:, b, :], bank(b)[:, 0:S], ACT.Gelu_apprx_tanh).then_inc(sem("gelu_done"), 1)

                act.wait_ge(sem("x_parked"), 16 * (s0 // NEXP) + 16)
                high_u(0, w0, first=True)
                high_u(1, w0 + 1)
                gelu(0, 0, True)
                high_v(0, w0 + 2, first=True)
                w1 = w0 + 3
                high_u(2, w1)
                gelu(1, 1, True)
                high_v(1, w1 + 1)
                high_u(3, w1 + 2)
                gelu(2, 0)
                high_v(2, w1 + 3)
                with act.Fori(1, (NEXP - 2) // 2) as i:
                    for b in range(2):
                        high_u(i * 2 + (b + 2), w1 + 2 * b, i)
                        gelu(i * 2 + (b + 1), 1 - b)
                        high_v(i * 2 + (b + 1), w1 + 2 * b + 1, i)
                gelu(NEXP - 1, 1)
                high_v(NEXP - 1, w1 + 2 * (NEXP - 2))

            def peer(p, off):
                norm(X[:, :, off:off + S], SQX2[:, :, 0:S], None)
                for s in range(4):
                    evacuate(8, lambda t, ps: copy(QT[:, t + 8 * s, :], ps[:, 0:S]))
                L.take("gate_args")
                L.give(f(TS, TS, ACT.Exp), "gate_exp")

                def gates(n, b, t0):
                    act.wait_ge(sem("gates_built"), n + 1)
                    copy(G[:, :, bass.ds(t0, 8)], PS(1024 * b, 8, P).rearrange("p t j -> p j t"))\
                        .then_inc(sem("gates_evacuated"), 1)

                with act.Fori(0, 16) as i:
                    for b in range(2):
                        gates(i * 2 + (32 * p + b), b, i * 16 + 8 * b)

                n0 = NEXP * p
                if p != 1:
                    split_experts(n0, NEXP * (p // 2), FIRST_ROW[p])
                    L.take("acc_evacuated")
                    return

                def gelu(j, b, first):
                    act.wait_ge(sem("up_ready"), j + (n0 + 1))
                    if not first:
                        act.wait_ge(sem("coef_ready"), j + (n0 - 1))
                    f(AC[:, b, :], bank(b)[:, 0:S], ACT.Gelu_apprx_tanh).then_inc(sem("gelu_done"), 1)


                def load_par(g):
                    act.dma_start(PARS, io["par"][:, bass.ds(g * NPAR, NPAR)]).then_inc(sem("par_loaded"), 16)

                def injection(g, first=False):
                    act.wait_ge(sem("inj_turned"), g + 1)
                    if not first:
                        act.wait_ge(sem("inj_stored"), g * 16)
                    copy(STGI, bank(6)[:, 0:S].rearrange("p (r m) -> p r m", r=2)).then_inc(sem("inj_evacuated"), 1)
                    act.wait_ge(sem("inj_evacuated"), g + 1)
                    act.dma_start(io["inj"][g], STGI.rearrange("p r m -> p (r m)")).then_inc(sem("inj_stored"), 16)
                    act.wait_ge(sem("cm_ready"), g + 1)
                    act.dma_start(io["cm"][g], WCM.rearrange("p r m -> p (r m)")).then_inc(sem("cm_stored"), 16)

                def lags(g, first=False):
                    act.wait_ge(sem("lags_turned"), g + 1)
                    if not first:
                        act.wait_ge(sem("lags_stored"), g * 32)
                    copy(STGK, bank(7)[:, 0:32].rearrange("p (m c) -> p m c", m=2)).then_inc(sem("lags_evacuated"), 1)
                    act.wait_ge(sem("lags_evacuated"), g + 1)
                    act.dma_start(io["lags"][g, 0:P], STGK[:, 0, :]).then_inc(sem("lags_stored"), 16)
                    act.dma_start(io["lags"][g, P:240], STGK[16:P, 1, :]).then_inc(sem("lags_stored"), 16)

                if p == 1:
                    act.wait_ge(sem("par_stored"), 16)
                    load_par(0)
                gelu(0, 0, True)
                gelu(1, 1, True)
                if p == 1:
                    injection(0, True)
                    lags(0, True)
                with act.Fori(1, NEXP // 2) as i:
                    if p == 1:
                        load_par(i)
                    for b in range(2):
                        gelu(i * 2 + b, b, False)
                        if p == 1:
                            (lags if b else injection)(i)
                L.take("acc_evacuated")

            act.wait_ge(sem("ssm_loaded"), 48)
            L.give(f(TP[:, 0, :], LAM[:, 2, :], ACT.Exp), "ssm_step")
            L.take("ssm_angle")
            L.do(f(TP[:, 6, :], TP[:, 1, :], ACT.Exp))
            L.do(f(TP[:, 7, :], TP[:, 4, :], ACT.Sin))
            L.give(f(TP[:, 8, :], TP[:, 5, :], ACT.Sin), "ssm_trig")
            with act.Fori(0, 6) as i:
                for b in range(2):
                    act.wait_ge(sem("ada_ready"), i * 2 + (b + 1))
                    copy(MR[:, i * 2 + b, :], PS(1024 * b, D, parts=2)).then_inc(sem("ada_evacuated"), 1)
            L.take("mods_used")
            norm(X, SQX2, None)
            evacuate(16, lambda t, ps: f(Z[:, t, :], ps, ACT.Gelu_apprx_tanh))
            L.take("centered")
            L.give(f(SQZ, Z[:, 8:16, :], ACT.Square), "squares")
            root(R1, R2)
            others(8)
            act.wait_ge(sem("lin_free"), L.lin)
            peer(0, 0)
            peer(1, S)
            norm(X, SQX2, None)
            evacuate(8, lambda t, ps: copy(UT[:, t, :], ps))
            for q in range(2):
                L.take("tokens_turned")
                for d in range(4):
                    last = copy(UN[:, 8 * (4 * q + d):8 * (4 * q + d) + 8, :, :].rearrange("p g s c -> p s g c"),
                                PS(1024 * d, 8, 8, 16, parts=64))
                L.give(last, "tokens_evacuated")
            L.take("groups_turned")
            L.give(copy(UG, PS(0, NG, 64)), "groups_ready")
            for q in range(8):
                L.take("injected")
                L.mark(copy(XS[:, :, :, 8 * q:8 * q + 8].rearrange("p n r g -> p g r n"),
                            PS(1024 * (q % 4), 8, 2, 64)), "injected_evacuated")
            for q in range(8):
                L.take("y_ready")
                L.mark(copy(YN[:, :, P * q:P * q + P].rearrange("p s (g c) -> p g s c", c=16),
                            PS(1024 * (q % 4), 8, 8, 16, parts=NCH)), "y_evacuated")
            L.take("y_summed")
            L.give(f(YT, YT, ACT.Gelu_apprx_tanh), "y_gelu")
            evacuate(8, lambda t, ps: f(SG[:, t, :], ps[:, 0:S], ACT.Sigmoid))
            others(8)
            act.wait_ge(sem("lin_free"), L.lin)
            peer(2, 0)
            norm(X[:, :, 0:S], SQX, None)

        @block.vector
        def _(dve):
            L = Line(dve, sem, sem("dve_chain"))
            tt, ts, stt, cp = dve.tensor_tensor, dve.tensor_scalar, dve.scalar_tensor_tensor, dve.tensor_copy

            def over(a, n, at):
                a = a.unsqueeze(at)
                shape = list(a.shape)
                shape[at] = n
                return a.to_broadcast(shape)

            def evacuate(tiles, fn, per):
                l0 = L.lin
                turns = L.loop(tiles // 2, 2 * per) if tiles >= 8 else [0]
                for i in turns:
                    for b in range(2):
                        dve.wait_ge(sem("lin_ready"), i * 2 + (l0 + b + 1))
                        fn(i * 2 + b, bank(b), b).then_inc(sem("lin_free"), 1)
                dve.wait_ge(sem("lin_free"), l0 + tiles)
                L.lin += tiles

            def others(tiles):
                L.lin += tiles

            def inv_var(scale, src, dst):
                L.take("rowsum")
                L.do(ts(dst, src, scale, EPS, ALU.mult, ALU.add))
                L.give(dve.reciprocal(dst, dst), "var")
                L.take("rstd")

            def norm(src, g, dst, kt, inv, n=S):
                inv_var(inv, bank(7)[:, 0:n], R1[:, 0:n])
                for k in range(kt):
                    last = stt(dst[:, k, :], src[:, k, :], g[:, k:k + 1], R2[:, 0:n], ALU.mult, ALU.mult)
                return last

            def scalar_of(name, t, k=0, per=1):
                return small[:, bass.ds(t * per + (COLS[name][0] + k), 1)]

            def conv(taps, name, dst):
                def fn(t, ps, b):
                    w = lambda j: scalar_of(name, t, j, taps)
                    L.do(ts(dst[:, t, :], ps[:, 0:S], w(taps - 1), None, ALU.mult))
                    for j in range(1, taps):
                        ins = stt(dst[:, t, j:S], ps[:, 0:S - j], w(taps - 1 - j), dst[:, t, j:S],
                                  ALU.mult, ALU.add)
                        if j < taps - 1:
                            L.do(ins)
                    return ins
                return fn

            dve.wait_ge(sem("inputs_loaded"), 64)
            L.give(norm(X[:, :, 0:S], col("norm_mix", 0, 8), H[:, :, 0:S], 8, 1.0 / D), "normed")
            evacuate(24, conv(4, "conv", QKV), 3)
            others(8)
            evacuate(8, lambda t, ps, b: cp(MISC[:, t, :], ps[:, 0:S]), 0)
            others(16)
            L.take("softplus_parts")
            L.do(stt(ROWS[:, 3, :], AB[0:8, :], 0.0, ROWS[:, 3, :], ALU.max, ALU.add))
            L.do(ts(ROWS[:, 3, :], ROWS[:, 3, :], TSUM[0:8, 0:1], -1.0, ALU.mult, ALU.mult))
            for c in range(2):
                t = slice(P * c, P * c + P)
                L.do(dve.tensor_tensor_scan(ROWS[:, 1, t], ones[0:8, :], ROWS[:, 3, t], 0.0, ALU.mult, ALU.add))
            for c in range(2):
                t = slice(P * c, P * c + P)
                ins = ts(ROWS[:, 3, t], ROWS[:, 1, t], -1.0, ROWS[:, 1, P * c + P - 1:P * c + P],
                         ALU.mult, ALU.add)
            L.give(ins, "decay_rows")
            L.take("head_sums")
            L.give(ts(SQ, PS(0, 16, S), EPS, None, ALU.add), "head_sums_used")
            L.give(dve.reciprocal(SQ, SQ), "head_var")
            L.take("head_rstd")
            stt(Q_, Q_, float(P) ** -0.5, SQ[:, 0:8, :], ALU.mult, ALU.mult)
            L.do(tt(K_, K_, SQ[:, 8:16, :], ALU.mult))
            L.take("rows_spread")
            L.give(cp(DEC, PS(2048, 8, S)), "decay_evacuated")
            L.take("exps_spread")
            L.do(ts(NGC, PS(2048, 2, 8), -1.0, None, ALU.mult))
            for h in range(NH):
                for c in range(2):
                    d = DEC[:, h, P * c:P * c + P]
                    ins = ts(d, d, NGC[:, c, h:h + 1], 0.0, ALU.add, ALU.min)
            L.give(ins, "decay_args")
            L.take("beta_evacuated")
            L.take("exps_evacuated")
            L.do(tt(V_, V_, BETA, ALU.mult))
            L.do(tt(KDC, K_[:, :, 0:P], EDB, ALU.mult))
            L.do(tt(QD, Q_[:, :, P:S], EGB, ALU.mult))
            L.do(tt(KBG, K_[:, :, P:S], BETA[:, :, P:S], ALU.mult))
            L.give(tt(KBG, KBG, EGB, ALU.mult), "gdn_operands")
            L.take("decay_exp")
            dec = DEC.rearrange("p h (c i) -> p (h c) i", c=2)
            L.do(tt(dec, dec, over(col1("causal"), 16, 1), ALU.mult))
            L.take("kk_ready")
            L.do(tt(LT, PS(0, 16, P), BETA.rearrange("p h (c i) -> p (h c) i", c=2), ALU.mult))
            L.do(tt(LT, LT, dec, ALU.mult))
            L.give(tt(AT, PS(2048, 16, P), dec, ALU.mult), "kk_evacuated")
            levels = col1("levels", LEVELS, P)
            L.do(tt(ML, LT, over(levels[:, 0, :], 16, 1), ALU.mult))
            L.give(stt(TT, ML, -1.0, over(ident, 16, 1), ALU.mult, ALU.add), "inverse_begun")
            L.take("inverse_turned")
            L.do(cp(TI, PS(0, 16, P)))
            for lev in range(1, LEVELS):
                L.give(tt(ML, LT, over(levels[:, lev, :], 16, 1), ALU.mult), "level_masked")
                L.take("level_inner")
                L.give(cp(AM, PS(0, 16, P)), "level_inner_evacuated")
                L.take("level_outer")
                L.do(tt(TT, TT, PS(0, 16, P), ALU.subtract))
                if lev < LEVELS - 1:
                    L.do(tt(TI, TI, PS(2048, 16, P), ALU.subtract))
            L.give(cp(TMAX, ident[:, 0:16]), "inverse_ready")
            L.take("new0_ready")
            L.give(cp(VN0, PS(0, 8, P)), "new0_evacuated")
            L.take("state_ready")
            L.do(cp(OG[:, :, 0:P], PS(2048, 8, P)))
            L.give(cp(S1, PS(1024, 8, P)), "state_evacuated")
            L.take("old_value_ready")
            L.give(tt(RR, VT.rearrange("p (h c) d -> p h c d", c=2)[:, :, 1, :], PS(0, 8, P), ALU.subtract),
                   "residual_ready")
            L.take("new1_ready")
            L.give(cp(VN1, PS(1024, 8, P)), "new1_evacuated")
            L.take("gdn_out1")
            L.give(cp(OG[:, :, P:S], PS(3072, 8, P)), "gdn_out")
            inv_var(1.0 / P, PS(0, 8, S), RSO)
            L.do(stt(OG, OG, col("gdn_norm"), RSO, ALU.mult, ALU.mult))
            L.give(tt(OG, OG, GT, ALU.mult), "gdn_gated")
            evacuate(8, lambda t, ps, b: tt(YA[:, t, :], ps[:, 0:S], GB[:, t, :], ALU.mult), 0)
            L.give(norm(CQ, col("q_norm", 0, 3), CQ, 3, 1.0 / 384), "latent_q_normed")
            L.give(norm(CKV, col("kv_norm", 0, 2), CKV, 2, 1.0 / 256), "latent_normed")
            others(8)
            evacuate(8, lambda t, ps, b: cp(QPR[:, t, :], ps[:, 0:S]), 0)
            cos, sin = col1("cos"), col1("sin")
            L.do(tt(TMP, QP, over(cos, 4, 1), ALU.mult))
            L.do(tt(QPS, QPS, over(sin, 4, 1), ALU.mult))
            L.do(tt(QP, TMP, QPS, ALU.add))
            L.do(tt(KP, KP, cos, ALU.mult))
            L.do(tt(KPS, KPS, sin, ALU.mult))
            L.do(dve.memset(KPP, 0.0))
            tt(KPP[0:64, 0, :], KP[0:64, :], KPS[0:64, :], ALU.add)
            L.give(tt(KPP[64:P, 1, :], KP[64:P, :], KPS[64:P, :], ALU.add), "rope_ready")
            others(8)
            L.take("scores_ready")
            sc = PS(0, 8, 512)
            scale = float(P + 64) ** -0.5
            neg = over(col1("neg"), 8, 1)
            stt(SC[:, :, 0:P], sc[:, :, 0:P], scale, neg, ALU.mult, ALU.add)
            ts(SC[:, :, P:S], sc[:, :, P:S], scale, None, ALU.mult)
            L.do(stt(SC[:, :, S:384], sc[:, :, S:384], scale, neg, ALU.mult, ALU.add))
            parts = ((slice(0, P), 0, P), (slice(P, 384), 8, S))
            for s, o, n in parts:
                L.do(dve.tensor_reduce(TMAX[:, o:o + 8], SC[:, :, s], AX, ALU.max))
            for s, o, n in parts:
                ins = tt(SC[:, :, s], SC[:, :, s], over(TMAX[:, o:o + 8], n, 2), ALU.subtract)
            L.give(ins, "scores_shifted")
            L.take("probs_exp")
            for s, o, n in parts:
                L.do(dve.tensor_reduce(TSUM[:, o:o + 8], SC[:, :, s], AX, ALU.add))
            L.do(dve.reciprocal(TSUM, TSUM))
            for s, o, n in parts:
                ins = tt(SC[:, :, s], SC[:, :, s], over(TSUM[:, o:o + 8], n, 2), ALU.mult)
            L.give(ins, "probs_ready")
            L.take("attention_out")
            L.give(cp(OB, PS(0, 8, S)), "attention_ready")

            def merge(t, ps, b):
                L.do(tt(TME[:, b, :], ps[:, 0:S], GB[:, t + 8, :], ALU.mult))
                return tt(MG[:, t, :], TME[:, b, :], YA[:, t, :], ALU.add)

            evacuate(8, merge, 1)
            add_x = lambda t, ps, b: tt(X[:, t, 0:S], ps[:, 0:S], X[:, t, 0:S], ALU.add)
            evacuate(8, add_x, 0)
            L.give(norm(X[:, :, 0:S], col("norm_ffn", 0, 8), H[:, :, 0:S], 8, 1.0 / D), "normed")
            evacuate(FT, conv(3, "conv_ffn", UF), 2)
            L.take("ffn_gate")
            L.give(tt(UF[:, 0:FK, :], UF[:, 0:FK, :], UF[:, FK:FT, :], ALU.mult), "ffn_inner")
            evacuate(8, add_x, 0)
            L.do(norm(X[:, :, 0:S], col("norm_final", 0, 8), X[:, :, 0:S], 8, 1.0 / D))
            dve.wait_ge(sem("pos_loaded"), 16)
            L.give(tt(X[:, :, 0:S], X[:, :, 0:S], H[:, :, S:2 * S], ALU.add), "x_normed")
            dve.wait_ge(sem("ssm_loaded"), 48)
            T = lambda k: TP[:, k, :]
            BBv = lambda r: PAR[:, :, PB_ + 16 * r:PB_ + 16 * r + 16]
            lr, li = LAM[:, 0, :], LAM[:, 1, :]
            L.take("ssm_step")
            L.do(tt(T(1), lr, T(0), ALU.mult))
            L.do(tt(T(2), li, T(0), ALU.mult))
            L.do(ts(T(3), T(2), 1.0 / TWO_PI, None, ALU.mult))
            L.do(ts(T(3), T(3), MAGIC, None, ALU.add))
            L.do(ts(T(3), T(3), MAGIC, None, ALU.subtract))
            L.do(stt(T(4), T(3), -C1, T(2), ALU.mult, ALU.add))
            L.do(stt(T(4), T(3), -C2, T(4), ALU.mult, ALU.add))
            L.do(stt(T(4), T(3), -C3, T(4), ALU.mult, ALU.add))
            L.do(ts(T(4), T(4), 3.1415925, -3.1415925, ALU.min, ALU.max))
            L.give(ts(T(5), T(4), 0.5, None, ALU.mult), "ssm_angle")
            L.take("ssm_trig")
            L.do(tt(T(9), T(8), T(8), ALU.mult))
            L.do(ts(T(9), T(9), -2.0, 1.0, ALU.mult, ALU.add))
            ar, ai = PW[:, 1, 0, :], PW[:, 1, 1, :]
            L.do(tt(ar, T(6), T(9), ALU.mult))
            L.do(tt(ai, T(6), T(7), ALU.mult))
            L.do(tt(T(10), lr, lr, ALU.mult))
            L.do(tt(T(11), li, li, ALU.mult))
            L.do(tt(T(10), T(10), T(11), ALU.add))
            L.do(dve.reciprocal(T(10), T(10)))
            L.do(ts(T(11), ar, -1.0, None, ALU.add))

            def cross(out, a, b, c, d, op, t1, t2):
                tt(t1, a, b, ALU.mult)
                L.do(tt(t2, c, d, ALU.mult))
                L.do(tt(out, t1, t2, op))

            cross(T(14), T(11), lr, ai, li, ALU.add, T(12), T(13))
            L.do(tt(T(14), T(14), T(10), ALU.mult))
            cross(T(15), ai, lr, T(11), li, ALU.subtract, T(12), T(13))
            L.do(tt(T(15), T(15), T(10), ALU.mult))
            cr, ci = over(T(14), 16, 2), over(T(15), 16, 2)
            cross(BBv(0), RAW[:, 0], cr, RAW[:, 1], ci, ALU.subtract, TB1, TB2)
            cross(BBv(1), RAW[:, 1], cr, RAW[:, 0], ci, ALU.add, TB1, TB2)
            dve.memset(PW[:, 0, 0, :], 1.0)
            dve.memset(PW[:, 0, 1, :], 0.0)
            cp(PAR[:, :, PC_:PC_ + 16], RAWC[:, 0])
            cp(PAR[:, :, PC_ + 16:PC_ + 32], RAWC[:, 1])
            L.do(ts(PAR[:, :, PC_ + 32:PC_ + 48], RAWC[:, 1], -1.0, None, ALU.mult))
            for j in range(2, 9):
                cross(PW[:, j, 0, :], PW[:, j - 1, 0, :], ar, PW[:, j - 1, 1, :], ai, ALU.subtract, T(12), T(13))
                cross(PW[:, j, 1, :], PW[:, j - 1, 0, :], ai, PW[:, j - 1, 1, :], ar, ALU.add, T(12), T(13))
            L.do(dve.memset(PAR[:, :, PM_:PM_ + 30], 0.0))
            F, B = slice(0, 64), slice(64, P)
            for r in range(2):
                for m in range(8):
                    for half, o, j in ((F, PM_ + 15 * r + m, 7 - m), (B, PM_ + 15 * r + 7 + m, m),
                                       (F, PI_ + 8 * r + m, 7 - m), (B, PI_ + 8 * r + m, m),
                                       (F, PO_ + 8 * r + m, m + 1), (B, PO_ + 8 * r + m, 8 - m)):
                        cp(PAR[half, :, o], PW[half, j, r, :])
            for r in range(2):
                cp(A1C[:, r, :], PW[:, 8, 0, :])
            ts(A2C[:, 0, :], PW[:, 8, 1, :], -1.0, None, ALU.mult)
            L.give(cp(A2C[:, 1, :], PW[:, 8, 1, :]), "par_ready")
            L.take("mods_ready")
            mod = MOD.rearrange("p l t c -> p (l t) c")
            L.give(tt(mod, PS(2048, 96, 2), over(col("ada_b", 0, 96), 2, 2), ALU.add), "mods_evacuated")
            for l in range(2):
                for w in range(2):
                    g = over(col("norm2" if w else "norm1", 8 * l, 8), 2, 2)
                    ins = stt(SA[:, l, w], MOD[:, l, 24 * w + 8:24 * w + 16, :], 1.0, g, ALU.add, ALU.mult)
            L.give(ins, "mods_used")

            def modulated(l, w, halves):
                n = S * halves
                inv_var(1.0 / D, bank(7)[:, 0:n], R1[:, 0:n])
                L.do(tt(H[:, :, 0:n], X[:, :, 0:n], over(R2[:, 0:n], 8, 1), ALU.mult))
                for c in range(halves):
                    for k in range(8):
                        h = H[:, k, S * c:S * c + S]
                        ins = ts(h, h, SA[:, l, w, k, c:c + 1], MOD[:, l, 24 * w + k, c:c + 1], ALU.mult, ALU.add)
                L.give(ins, "normed")

            def top16(rows):
                steps = (lambda v, x, s, w: dve.max(v[:, 0:8], s),
                         lambda v, x, s, w: dve.max_index(x[:, 0:8], v[:, 0:8], s),
                         lambda v, x, s, w: dve.match_replace(w, v[:, 0:8], s, LOWEST),
                         lambda v, x, s, w: dve.max(v[:, 8:16], w),
                         lambda v, x, s, w: dve.max_index(x[:, 8:16], v[:, 8:16], w))
                for step in steps:
                    for row in rows[:-1]:
                        step(*row)
                    L.do(step(*rows[-1]))

            def split_experts(n0, s0, w0):
                def low(u, j, w):
                    name = "uv"[u]
                    dve.wait_ge(sem(name + "_high"), j + (s0 + 1))
                    tt(SPL[:, u, 1, :], ring[:, w % RING, :], SPL[:, u, 0, :].bitcast(F32), ALU.subtract)\
                        .then_inc(sem(name + "_low"), 1)

                def coef(j, b, first=False):
                    dve.wait_ge(sem("gelu_done"), j + (n0 + 1))
                    L.do(tt(CT[:, b, :], AC[:, b, :], G[:, j, :], ALU.mult))
                    if not first:
                        dve.wait_ge(sem("coef_used"), j + (n0 - 1))
                    L.do(cp(CFR[:, b, 0, :], CT[:, b, :]))
                    tt(CFR[:, b, 1, :], CT[:, b, :], CFR[:, b, 0, :].bitcast(F32), ALU.subtract)\
                        .then_inc(sem("coef_ready"), 1)

                low(0, 0, w0)
                low(0, 1, w0 + 1)
                coef(0, 0, True)
                low(1, 0, w0 + 2)
                w1 = w0 + 3
                low(0, 2, w1)
                coef(1, 1, True)
                low(1, 1, w1 + 1)
                low(0, 3, w1 + 2)
                coef(2, 0)
                low(1, 2, w1 + 3)
                for i in L.loop((NEXP - 2) // 2 - 1, 4):
                    for b in range(2):
                        low(0, i * 2 + (b + 4), w1 + 2 * b)
                        coef(i * 2 + (b + 3), 1 - b)
                        low(1, i * 2 + (b + 3), w1 + 2 * b + 1)
                coef(NEXP - 1, 1)
                low(1, NEXP - 1, w1 + 2 * (NEXP - 2))

            def peer(p, l, off, c):
                inv_var(1.0 / D, bank(7)[:, 0:S], R1[:, 0:S])
                ht = HT if p != 1 else H[:, :, 0:S]
                L.do(tt(ht, X[:, :, off:off + S], over(R2[:, 0:S], 8, 1), ALU.mult))
                for k in range(8):
                    ins = ts(ht[:, k, :], ht[:, k, :], SA[:, l, 1, k, c:c + 1], MOD[:, l, 24 + k, c:c + 1],
                             ALU.mult, ALU.add)
                L.give(ins, "normed")
                if p != 1:
                    L.do(cp(HR[:, 0], HT))
                    L.give(tt(HR[:, 1], HT, HR[:, 0].bitcast(F32), ALU.subtract), "input_parts")
                sv = SV.rearrange("p i (h k) a -> p i h k a", k=2)
                cand = CAND.rearrange("p (i h) (a b) -> p i h a b", i=2, a=16)
                for s in range(4):
                    others(8)
                    L.take("key_scores")
                    top16([(SV[:, i, 4 * s + q, :], IDX[:, i, 4 * s + q, :],
                            bank(2 + 2 * (s % 2) + i)[:, P * q:P * q + P], WK[:, 4 * i + q, :])
                           for i in range(2) for q in range(4)])
                    hs = slice(2 * s, 2 * s + 2)
                    for i in range(2):
                        ins = tt(cand[:, i, hs], over(sv[:, i, hs, 0, :], 16, 3), over(sv[:, i, hs, 1, :], 16, 2),
                                 ALU.add)
                    L.give(ins, "key_scores_used")
                    top16([(TS[:, 8 * i + h, :], TC[:, 8 * i + h, :], CAND[:, 8 * i + h, :], WK2[:, 2 * i + h - 2 * s, :])
                           for i in range(2) for h in (2 * s, 2 * s + 1)])
                tc = TC.rearrange("p h k -> p (h k)")
                L.do(ts(CI[:, 0, :], tc, 4, None, ALU.logical_shift_right))
                L.do(ts(CI[:, 1, :], tc, 15, None, ALU.bitwise_and))
                L.do(cp(CF_, CI))
                L.do(cp(IDF, IDX))
                idf = IDF.rearrange("p i (h k) a -> p (i h) k a", k=2)
                oh = OH.rearrange("p (h k) a -> p h k a", h=16)
                for m in range(2):
                    L.do(tt(OH, over(CF_[:, m, :], 16, 2), over(iota[:, 0:16], 256, 1), ALU.is_equal))
                    L.do(tt(oh, oh, over(idf[:, :, m, :], 16, 2), ALU.mult))
                    L.do(dve.tensor_reduce(KK[:, m, :], OH, AX, ALU.add))
                L.do(tt(oh[:, 0, :, :], TS, over(TS[:, :, 0], 16, 2), ALU.subtract))
                L.give(cp(TS, oh[:, 0, :, :]), "gate_args")
                L.take("gate_exp")
                L.do(dve.tensor_reduce(TSUM, TS, AX, ALU.add))
                L.do(dve.reciprocal(TSUM, TSUM))
                L.give(tt(KK[:, 2, :].rearrange("p (h k) -> p h k", h=16), TS, over(TSUM, 16, 2), ALU.mult),
                       "chosen")
                L.take("chosen_turned")
                L.give(cp(K3, PS(0, 3, S)), "chosen_evacuated")

                def onehots(n, b, t0, first):
                    if not first:
                        dve.wait_ge(sem("gates_built"), n - 1)
                    L.do(cp(KS[:, b], K3[:, :, bass.ds(t0, 8)]))
                    for t in range(8):
                        k = lambda m: KS[:, b, m, t:t + 1]
                        ts(EA[:, b, t, :], iota, k(0), k(2), ALU.is_equal, ALU.mult)
                        last = ts(EB[:, b, t, :], iota, k(1), None, ALU.is_equal)
                    last.then_inc(sem("onehots_ready"), 1)

                for b in range(2):
                    onehots(32 * p + b, b, 8 * b, True)
                for i in L.loop(15, 2):
                    for b in range(2):
                        onehots(i * 2 + (32 * p + 2 + b), b, i * 16 + (16 + 8 * b), False)

                n0 = NEXP * p

                def coef(j, b, first):
                    dve.wait_ge(sem("gelu_done"), j + (n0 + 1))
                    if not first:
                        dve.wait_ge(sem("coef_used"), j + (n0 - 1))
                    tt(CF[:, b, :], AC[:, b, :], G[:, j, :], ALU.mult).then_inc(sem("coef_ready"), 1)

                dve.wait_ge(sem("gates_evacuated"), 32 * p + 32)
                RE, IM = ((0, 0), (1, 1), ALU.subtract), ((0, 1), (1, 0), ALU.add)

                def outer(out, pw, mat, n, how):
                    a = [over(PARS[:, pw + n * r:pw + n * r + n], 16, 2) for r in range(2)]
                    m = [over(PARS[:, mat + 16 * r:mat + 16 * r + 16], n, 1) for r in range(3 if mat == PC_ else 2)]
                    t1 = WT1[:, 0:16 * n].rearrange("p (n c) -> p n c", c=16)
                    t2 = WT2[:, 0:16 * n].rearrange("p (n c) -> p n c", c=16)
                    (p1, m1), (p2, m2), op = how
                    tt(t1, a[p1], m[m1], ALU.mult)
                    L.do(tt(t2, a[p2], m[m2], ALU.mult))
                    return tt(out.rearrange("p (n c) -> p n c", c=16), t1, t2, op)

                def injection(g, first=False):
                    dve.wait_ge(sem("par_loaded"), g * 16 + 16)
                    if not first:
                        dve.wait_ge(sem("inj_turned"), g)
                        dve.wait_ge(sem("cm_stored"), g * 16)
                    L.do(outer(WCI[:, 0, :], PI_, PB_, 8, RE))
                    outer(WCI[:, 1, :], PI_, PB_, 8, IM).then_inc(sem("inj_ready"), 1)
                    dve.wait_ge(sem("inj_ready"), g + 1)
                    L.do(outer(WCM[:, 0, :], PO_, PC_, 8, RE))
                    outer(WCM[:, 1, :], PO_, PC_, 8, ((0, 2), (1, 0), ALU.subtract)).then_inc(sem("cm_ready"), 1)
                    dve.wait_ge(sem("cm_ready"), g + 1)

                def lags(g, first=False):
                    if not first:
                        dve.wait_ge(sem("lags_turned"), g)
                    L.do(outer(WW[:, 0, :], PM_, PB_, 15, RE))
                    outer(WW[:, 1, :], PM_, PB_, 15, IM).then_inc(sem("lags_ready"), 1)
                    dve.wait_ge(sem("lags_ready"), g + 1)

                if p != 1:
                    split_experts(n0, NEXP * (p // 2), FIRST_ROW[p])
                    dve.wait_ge(sem("x_back"), 16 * (p // 2) + 16)
                else:
                    coef(0, 0, True)
                    coef(1, 1, True)
                    injection(0, True)
                    lags(0, True)
                    for i in L.loop(NEXP // 2 - 1, 9):
                        for b in range(2):
                            coef(i * 2 + (2 + b), b, False)
                            (lags if b else injection)(i + 1)
                    dve.wait_ge(sem("inj_stored"), 16 * NG)
                    dve.wait_ge(sem("cm_stored"), 16 * NG)
                    dve.wait_ge(sem("lags_stored"), 32 * NG)
                dve.wait_ge(sem("coef_used"), NEXP * p + NEXP)
                for d in range(8):
                    x = X[:, d, off:off + S]
                    ins = stt(x, PS(1024 + S * d, S), MOD[:, l, 40 + d, c:c + 1], x, ALU.mult, ALU.add)
                L.give(ins, "acc_evacuated")

            modulated(0, 0, 2)
            others(16)
            L.take("rowsum")
            L.do(ts(R1, bank(7), 1.0 / D, None, ALU.mult))
            zv = Z[:, 8:16, :]
            L.give(tt(zv, zv, over(R1, 8, 1), ALU.subtract), "centered")
            inv_var(1.0 / D, bank(7), R1)
            L.do(tt(zv, zv, over(R2, 8, 1), ALU.mult))
            for k in range(8):
                ins = ts(zv[:, k, :], zv[:, k, :], col("ln_g", k), col("ln_b", k), ALU.mult, ALU.add)
            L.give(ins, "v_normed")
            L.take("v_turned")
            L.give(cp(ZT, PS(0, 32, P)), "v_turned_evacuated")
            L.take("mixed")
            L.give(tt(Z[:, 0:8, :], Z[:, 0:8, :], PS(0, 8, 512), ALU.mult), "mixed_used")

            def add_gated(t, ps, b):
                for c in range(2):
                    x = X[:, t, S * c:S * c + S]
                    g = small[:, bass.ds(t * 2 + (T0 + 2 * 16 + c), 1)]
                    ins = stt(x, ps[:, S * c:S * c + S], g, x, ALU.mult, ALU.add)
                return ins

            evacuate(8, add_gated, 0)
            dve.wait_ge(sem("par_stored"), 16)
            peer(0, 0, 0, 0)
            peer(1, 0, S, 1)
            modulated(1, 0, 2)
            others(8)
            F, B = slice(0, 64), slice(64, P)
            dve.wait_ge(sem("injected_evacuated"), 8)
            h = HST
            L.do(dve.memset(h, 0.0))

            def step(fwd, bwd):
                tt(ST1, A1C, h, ALU.mult)
                tt(ST2[:, 0, :], A2C[:, 0, :], h[:, 1, :], ALU.mult)
                L.do(tt(ST2[:, 1, :], A2C[:, 1, :], h[:, 0, :], ALU.mult))
                L.do(tt(ST1, ST1, ST2, ALU.add))
                tt(h[F], ST1[F], XS[F, fwd], ALU.add)
                L.do(tt(h[B], ST1[B], XS[B, bwd], ALU.add))

            for i in L.loop(NCH, 3):
                step(i + NCH, i * -1 + (2 * NCH - 1))
            for i in L.loop(NCH, 4):
                cp(HS[F, i], h[F])
                L.do(cp(HS[B, i * -1 + (NCH - 1)], h[B]))
                step(i, i * -1 + (NCH - 1))
            L.give(cp(TMAX, ident[:, 0:16]), "scanned")

            L.take("y_turned")
            yp = PS(0, 8, 8, NCH).rearrange("p d s n -> p d n s")
            for d in range(8):
                ins = stt(YT[:, d, :].rearrange("p (n s) -> p n s", s=8),
                          UT[:, d, 0:S].rearrange("p (n s) -> p n s", s=8), col("ssm_d", d), yp[:, d],
                          ALU.mult, ALU.add)
            L.give(ins, "y_summed")
            others(8)

            def glu(t, ps, b):
                L.do(tt(TMPX[:, b, :], ps[:, 0:S], SG[:, t, :], ALU.mult))
                g = small[:, bass.ds(t * 2 + (T0 + 96 + 2 * 16), 1)]
                return stt(X[:, t, 0:S], TMPX[:, b, :], g, X[:, t, 0:S], ALU.mult, ALU.add)

            evacuate(8, glu, 1)
            peer(2, 1, 0, 0)
            L.give(norm(X[:, :, 0:S], col("final", 0, 8), out_t, 8, 1.0 / D), "result_ready")


FIRST_ROW = (SEGS["q0"][0] + 36, SEGS["q0"][0] + 72 + 2 * NEXP, SEGS["q0"][0] + 132 + 4 * NEXP)
SLOTS_READ = SEGS["q0"][0] + 36 + 2 * NEXP + 36 + 2 * NEXP + 60 + 2 * NEXP


def shape_constants():
    f = np.float32
    i = np.arange(P)
    half = 32
    inv = (10000.0 ** (-np.arange(half, dtype=f) / f(half))).astype(f)
    ang = np.arange(S, dtype=f)[None, :] * inv[:, None]
    cos, sin = np.cos(ang), np.sin(ang)
    levels = []
    for lev in range(LEVELS):
        m = 1 << lev
        levels.append(((i[:, None] // (2 * m) == i[None, :] // (2 * m)) & (i[None, :] % (2 * m) >= m)
                       & (i[:, None] % (2 * m) < m)).astype(f))
    sel = np.zeros((P, NH, P), f)
    for h in range(NH):
        sel[h, h, :] = 1.0
    cols1 = np.concatenate([
        np.tile(cos, (4, 1)), np.concatenate([-sin, sin, -sin, sin]),
        np.where(i[:, None] >= i[None, :], 0.0, -1.0e30), (i[None, :] >= i[:, None]),
        np.concatenate(levels, 1), sel.reshape(P, -1)], 1).astype(f)
    omega = (1.0 / (10000.0 ** (np.arange(256, dtype=f) / f(256)))).astype(f)
    t = np.arange(S)
    emb = []
    for pos in (t // 64, t % 64):
        a = pos.astype(f)[:, None] * omega[None, :]
        emb += [np.sin(a), np.cos(a)]
    pos = np.concatenate(emb, 1).T.reshape(KD_, P, S).transpose(1, 0, 2).astype(f)
    return np.ascontiguousarray(cols1), np.ascontiguousarray(pos)


def lay_out(a):
    f = np.float32

    def tiles(w):
        k, n = w.shape
        return w.reshape(k // P, P, n // P, P).transpose(2, 0, 1, 3).reshape(-1, P, P)

    def slots(t):
        assert t.shape[0] % 8 == 0, t.shape
        return t.reshape(-1, 8, P, P).transpose(0, 2, 1, 3).reshape(-1, P, SLOT)

    w = a["w_in"][0]
    o = np.cumsum([0, 3072, 1024, 8, 8, 384, 256, 64, 1024, 1024])
    part = [w[:, o[i]:o[i + 1]] for i in range(9)]
    ab = np.zeros((D, P), f)
    ab[:, 0:8], ab[:, 32:40] = part[2], part[3]
    kpe = part[6]
    swap = lambda m: np.concatenate([m[..., 32:], m[..., :32]], -1)
    w_in = np.concatenate([part[0], part[1], ab, part[4], part[5], kpe, kpe, swap(kpe), swap(kpe),
                           part[7], part[8]], 1)
    uq = a["w_uq"][0].reshape(384, NH, 192)
    pe = uq[:, :, 128:]
    w_uq = np.concatenate([uq[:, :, :128].reshape(384, -1), pe.reshape(384, -1), swap(pe).reshape(384, -1)], 1)
    ukv = a["w_ukv"][0].reshape(256, NH, 256)
    seg = {
        "in": slots(tiles(w_in)), "o_gdn": slots(tiles(a["w_o_gdn"][0])), "uq": slots(tiles(w_uq)),
        "kn": slots(tiles(ukv[:, :, :128].reshape(256, -1))), "v": ukv[:, :, 128:].reshape(2, P, D),
        "o_mla": slots(tiles(a["w_o_mla"][0])), "out": slots(tiles(a["w_out"][0])),
        "up": slots(tiles(a["w_up"][0])), "down": slots(tiles(a["w_down"][0])),
        "ada": a["ada_w_2"].reshape(2, 8, P, 6, D).transpose(0, 3, 1, 2, 4).reshape(96, P, D),
        "cm_in": slots(tiles(a["cm_w_in_2"][0])),
        "ws": a["cm_w_s_2"][0].transpose(2, 0, 1).reshape(1, P, D),
        "cm_out": slots(tiles(a["cm_w_out_2"][0])),
        "ssm_in": slots(tiles(a["ssm_w_in_2"][0])),
        "ssm_out": slots(tiles(np.concatenate([a["ssm_w_out_2"][0][:, D:], a["ssm_w_out_2"][0][:, :D]], 1))),
    }
    for l in range(2):
        keys = a["peer_keys_2"][l].reshape(16, P, 2, P).transpose(0, 2, 3, 1).reshape(32, P, P)
        q = slots(tiles(a["peer_w_q_2"][l])).reshape(4, 8, P, SLOT)
        seg[f"q{l}"] = np.concatenate([q, slots(keys)[:, None]], 1).reshape(36, P, SLOT)
    stream = np.concatenate([seg[n] for n in SEGS])
    for n, (b, c) in SEGS.items():
        assert seg[n].shape == (c, P, SLOT), (n, seg[n].shape)

    by_feature = lambda v: v.reshape(-1, P).T
    taps = lambda v: v.reshape(v.shape[0], -1, P).transpose(2, 1, 0).reshape(P, -1)
    head_col = lambda v: np.concatenate([v, np.zeros(P - NH, f)]).reshape(P, 1)
    cond = np.stack([a["c_2"][0], a["c_ctx_2"]], -1).reshape(KD_, P, 2).transpose(1, 0, 2).reshape(P, 16)
    cols = {
        "ident": np.eye(P, dtype=f), "ones": np.ones((P, P), f),
        "iota": np.tile(np.arange(P, dtype=f), (P, 1)), "norm_mix": by_feature(a["norm_mix_g"][0]),
        "conv": taps(a["conv_qkv_w"][0]), "gdn_norm": by_feature(a["gdn_norm_g"][0]),
        "a_log": head_col(a["gdn_a_log"][0]), "dt_bias": head_col(a["gdn_dt_bias"][0]),
        "q_norm": by_feature(a["mla_q_norm_g"][0]), "kv_norm": by_feature(a["mla_kv_norm_g"][0]),
        "norm_ffn": by_feature(a["norm_ffn_g"][0]), "conv_ffn": taps(a["conv_ffn_w"][0]),
        "norm_final": by_feature(a["norm_final_g"]), "ada_b": by_feature(a["ada_b_2"].reshape(-1)),
        "norm1": by_feature(a["norm1_g_2"].reshape(-1)), "norm2": by_feature(a["norm2_g_2"].reshape(-1)),
        "final": by_feature(a["final_g_2"]), "ln_g": by_feature(a["cm_ln_g_2"][0]),
        "ln_b": by_feature(a["cm_ln_b_2"][0]), "ssm_d": by_feature(a["ssm_d_2"][0]), "cond": cond,
    }
    for n, (b, c) in COLS.items():
        assert cols[n].shape == (P, c), n
    cols1, pos = shape_constants()
    feat = lambda x: x[0].T.reshape(KD_, P, S).transpose(1, 0, 2)
    states = lambda v: v.transpose(0, 2, 1).reshape(P, NG)
    mats = lambda v: v.transpose(0, 2, 1, 3).reshape(P, NG, 16)
    lam = np.stack([states(a["ssm_lam_re_2"][0]), states(a["ssm_lam_im_2"][0]),
                    np.repeat(a["ssm_log_step_2"][0][:, None, :], 64, 1).reshape(P, NG)], 1)
    ssm_b = np.stack([mats(a["ssm_b_re_2"][0]), mats(a["ssm_b_im_2"][0])], 1)
    ssm_c = np.stack([mats(a["ssm_c_re_2"][0].transpose(0, 1, 3, 2)),
                      mats(a["ssm_c_im_2"][0].transpose(0, 1, 3, 2))], 1)
    u = a["peer_u_2"].reshape(2, NEXP, P, KD_, P).transpose(0, 1, 4, 3, 2).reshape(2, NEXP, P, SLOT)
    v = a["peer_v_2"].reshape(2, NEXP, P, SLOT)
    out = {"x": feat(a["x"]), "ctx": feat(a["ctx_2"]), "cols": np.concatenate([cols[n] for n in COLS], 1),
           "cols1": cols1, "pos": pos, "bs": a["cm_b_s_2"][0].reshape(1, D), "ssm_lam": lam, "ssm_b": ssm_b,
           "ssm_c": ssm_c, "w": stream, "u": u, "v": v}
    return {n: np.ascontiguousarray(x) for n, x in out.items()}


def kernel(**inputs):
    import concourse.bacc as bacc
    from concourse.bass_utils import run_bass_kernel_spmd

    nc = bacc.Bacc("TRN2", target_bir_lowering=False, num_devices=1)
    arrays = lay_out({n: np.asarray(v) for n, v in inputs.items()})
    io = {n: nc.dram_tensor(f"in_{n}", x.shape, mybir.dt.from_np(x.dtype), kind="ExternalInput").ap()
          for n, x in arrays.items()}
    io["out"] = nc.dram_tensor("out_x", (P, KD_, S), F32, kind="ExternalOutput").ap()
    for n, shape in (("parked", (P, KD_ * 2 * S)), ("par", (P, NG * NPAR)), ("inj", (NG, P, S)), ("cm", (NG, P, S)), ("lags", (NG, 240, 16))):
        io[n] = nc.dram_tensor(f"scratch_{n}", shape, F32, kind="Internal").ap()
    build(nc, io)
    r = run_bass_kernel_spmd(nc, [{f"in_{n}": x for n, x in arrays.items()}], core_ids=[0])
    return r.results[0]["out_x"].transpose(1, 0, 2).reshape(1, D, S).transpose(0, 2, 1)
```
